# Optimizing a Trainium2 kernel written in Bass

```python
import jax, jax.numpy as jnp
from jax import lax
import numpy as np

D_MODEL = 1024
BATCH = 1
SEQ = 512
DEPTH = 1

HG_HEADS = 4
HG_DK = 128
HG_DV = 128
HG_WIDTH = HG_HEADS * HG_DK
HG_CHUNK = 64

ATT_HEADS = 8
ATT_GROUPS = 2
ATT_HEAD_DIM = 64
ATT_REP = ATT_HEADS // ATT_GROUPS
ATT_WIDTH = ATT_HEADS * ATT_HEAD_DIM
ATT_KV_WIDTH = ATT_GROUPS * ATT_HEAD_DIM
IDX_HEADS = 8
IDX_DIM = 64
IDX_TOPK_MAX = 256
Q_BLOCK = 128

PEER_HEADS = 8
PEER_NKEYS = 128
PEER_NEXP = PEER_NKEYS * PEER_NKEYS
PEER_DKEY = 256
PEER_TOPK = 16
PEER_TOK_BLOCK = 128

RMS_EPS = 1e-6

IN_SPLIT = (HG_WIDTH, HG_WIDTH, HG_WIDTH, HG_WIDTH,
            ATT_WIDTH, ATT_KV_WIDTH, ATT_KV_WIDTH,
            IDX_HEADS * IDX_DIM, IDX_DIM, IDX_HEADS,
            D_MODEL, D_MODEL)
IN_WIDTH = 4 * HG_WIDTH + ATT_WIDTH + 2 * ATT_KV_WIDTH + IDX_HEADS * IDX_DIM + IDX_DIM + IDX_HEADS + 2 * D_MODEL

kernel_name = 'hybrid_hgrn2_dsa_peer_block'

def rmsnorm(x, g):
    xf = x.astype(jnp.float32)
    y = xf * lax.rsqrt(jnp.mean(xf * xf, axis=-1, keepdims=True) + RMS_EPS)
    return (y * g.astype(jnp.float32)).astype(x.dtype)

def alibi_slopes(n_heads):
    return jnp.exp2(-8.0 * (jnp.arange(n_heads, dtype=jnp.float32) + 1.0) / n_heads)

def hgrn2_mix(q, f_pre, i, g, lb, onorm_g):
    B, S, _ = q.shape
    C = HG_CHUNK
    N = S // C
    dt = q.dtype

    def heads(t):
        return t.astype(jnp.float32).reshape(B, N, C, HG_HEADS, -1).transpose(0, 3, 1, 2, 4)

    lbf = lb.astype(jnp.float32).reshape(HG_HEADS, 1, 1, HG_DK)
    qh = jax.nn.silu(heads(q))
    f = lbf + (1.0 - lbf) * jax.nn.sigmoid(heads(f_pre))
    kh = 1.0 - f
    vh = heads(i)
    b = jnp.cumsum(jnp.log(f), axis=3)
    b_mid = b[:, :, :, C // 2 - 1:C // 2]
    b_last = b[:, :, :, -1:]
    A = jnp.einsum('bhncd,bhnsd->bhncs', qh * jnp.exp(b - b_mid), kh * jnp.exp(b_mid - b))
    causal = jnp.tril(jnp.ones((C, C), dtype=bool))
    A = jnp.where(causal, A, 0.0)
    o = jnp.einsum('bhncs,bhnse->bhnce', A, vh)
    dS = jnp.einsum('bhnsd,bhnse->bhnde', kh * jnp.exp(b_last - b), vh)
    decay = jnp.exp(b_last[:, :, :, 0])

    def step(S_prev, inp):
        dec, ds = inp
        return dec[..., None] * S_prev + ds, S_prev

    S0 = jnp.zeros((B, HG_HEADS, HG_DK, HG_DV), jnp.float32)
    _, S_before = lax.scan(step, S0, (jnp.moveaxis(decay, 2, 0), jnp.moveaxis(dS, 2, 0)))
    S_before = jnp.moveaxis(S_before, 0, 2)
    o = o + jnp.einsum('bhncd,bhnde->bhnce', qh * jnp.exp(b), S_before)
    o = rmsnorm(o, onorm_g) * jax.nn.silu(heads(g))
    return o.transpose(0, 2, 3, 1, 4).reshape(B, S, HG_WIDTH).astype(dt)

def dsa_mix(q, k, v, q_idx, k_idx, w_idx):
    B, S = q.shape[0], q.shape[1]
    topk = min(IDX_TOPK_MAX, S // 4)
    nb = S // Q_BLOCK
    slopes = alibi_slopes(ATT_HEADS).reshape(ATT_GROUPS, ATT_REP)
    kpos = jnp.arange(S)
    idx_scale = (IDX_DIM ** -0.5) * (IDX_HEADS ** -0.5)
    att_scale = ATT_HEAD_DIM ** -0.5

    def to_blocks(t):
        return jnp.moveaxis(t.reshape(B, nb, Q_BLOCK, *t.shape[2:]), 1, 0)

    def block(args):
        qb, qib, wb, t0 = args
        tpos = t0 + jnp.arange(Q_BLOCK)
        s = jnp.einsum('bqhd,bsd->bqhs', qib, k_idx)
        I = jnp.einsum('bqh,bqhs->bqs', wb, jax.nn.relu(s)).astype(jnp.float32) * idx_scale
        causal = kpos[None, :] <= tpos[:, None]
        I = jnp.where(causal[None], I, -jnp.inf)
        _, sel = lax.top_k(I, topk)
        valid = sel <= tpos[None, :, None]
        kg = jax.vmap(lambda kk, ii: kk[ii])(k, sel)
        vg = jax.vmap(lambda vv, ii: vv[ii])(v, sel)
        qg = qb.reshape(B, Q_BLOCK, ATT_GROUPS, ATT_REP, ATT_HEAD_DIM)
        sc = jnp.einsum('bqgrd,bqkgd->bqgrk', qg, kg).astype(jnp.float32) * att_scale
        dist = (tpos[None, :, None] - sel).astype(jnp.float32)
        sc = sc - slopes[None, None, :, :, None] * dist[:, :, None, None, :]
        sc = jnp.where(valid[:, :, None, None, :], sc, -jnp.inf)
        p = jax.nn.softmax(sc, axis=-1).astype(vg.dtype)
        o = jnp.einsum('bqgrk,bqkgd->bqgrd', p, vg)
        return o.reshape(B, Q_BLOCK, ATT_WIDTH)

    out = lax.map(block, (to_blocks(q), to_blocks(q_idx), to_blocks(w_idx),
                          jnp.arange(nb, dtype=jnp.int32) * Q_BLOCK))
    return jnp.moveaxis(out, 0, 1).reshape(B, S, ATT_WIDTH)

def peer_ffn(h, wq, subkeys, u, vtab):
    B, S, D = h.shape
    T = B * S
    hf = h.reshape(T, D)
    qry = (hf @ wq).reshape(T, PEER_HEADS, 2, PEER_DKEY // 2)
    sc = jnp.einsum('thpd,hpnd->thpn', qry, subkeys).astype(jnp.float32)
    s1, i1 = lax.top_k(sc[:, :, 0], PEER_TOPK)
    s2, i2 = lax.top_k(sc[:, :, 1], PEER_TOPK)
    cand = (s1[..., :, None] + s2[..., None, :]).reshape(T, PEER_HEADS, PEER_TOPK * PEER_TOPK)
    cidx = (i1[..., :, None] * PEER_NKEYS + i2[..., None, :]).reshape(T, PEER_HEADS, PEER_TOPK * PEER_TOPK)
    top_s, pos = lax.top_k(cand, PEER_TOPK)
    eidx = jnp.take_along_axis(cidx, pos, axis=-1)
    gates = jax.nn.softmax(top_s, axis=-1).astype(h.dtype)
    nb = T // PEER_TOK_BLOCK

    def block(args):
        xb, eb, gb = args
        a = jax.nn.gelu(jnp.einsum('td,thkd->thk', xb, u[eb]), approximate=False)
        return jnp.einsum('thk,thkd->td', gb * a, vtab[eb])

    out = lax.map(block, (hf.reshape(nb, PEER_TOK_BLOCK, D),
                          eidx.reshape(nb, PEER_TOK_BLOCK, PEER_HEADS, PEER_TOPK),
                          gates.reshape(nb, PEER_TOK_BLOCK, PEER_HEADS, PEER_TOPK)))
    return out.reshape(B, S, D)

def setup_inputs(seed: int = 0) -> dict:
    key = jax.random.key(seed)
    ks = jax.random.split(key, 18)
    n = jax.random.normal
    L, D = DEPTH, D_MODEL
    f32 = jnp.float32
    return {
        'x': n(ks[0], (BATCH, SEQ, D), f32),
        'c': n(ks[1], (BATCH, D), f32),
        'w_ada': n(ks[2], (L, D, 6 * D), f32) * (0.5 * D ** -0.5),
        'b_ada': n(ks[3], (L, 6 * D), f32) * 0.01,
        'norm1_g': 1.0 + 0.02 * n(ks[4], (L, D), f32),
        'norm2_g': 1.0 + 0.02 * n(ks[5], (L, D), f32),
        'w_in': n(ks[6], (L, D, IN_WIDTH), f32) * D ** -0.5,
        'hg_lb': 0.1 * n(ks[7], (L + 1, HG_WIDTH), f32),
        'hg_onorm_g': 1.0 + 0.02 * n(ks[8], (L, HG_DV), f32),
        'q_norm_g': 1.0 + 0.02 * n(ks[9], (L, ATT_HEAD_DIM), f32),
        'k_norm_g': 1.0 + 0.02 * n(ks[10], (L, ATT_HEAD_DIM), f32),
        'w_a': n(ks[11], (L, HG_WIDTH, D), f32) * HG_WIDTH ** -0.5,
        'w_b': n(ks[12], (L, ATT_WIDTH, D), f32) * ATT_WIDTH ** -0.5,
        'w_out': n(ks[13], (L, D, D), f32) * D ** -0.5,
        'peer_wq': n(ks[14], (L, D, PEER_HEADS * PEER_DKEY), f32) * D ** -0.5,
        'peer_subkeys': n(ks[15], (L, PEER_HEADS, 2, PEER_NKEYS, PEER_DKEY // 2), f32) * (PEER_DKEY // 2) ** -0.5,
        'peer_u': n(ks[16], (L, PEER_NEXP, D), f32) * D ** -0.5,
        'peer_v': n(ks[17], (L, PEER_NEXP, D), f32),
    }

def reference(x, c, w_ada, b_ada, norm1_g, norm2_g, w_in, hg_lb, hg_onorm_g, q_norm_g, k_norm_g,
              w_a, w_b, w_out, peer_wq, peer_subkeys, peer_u, peer_v):
    B, S, D = x.shape
    lb_all = jnp.cumsum(jax.nn.softmax(hg_lb.astype(jnp.float32), axis=0), axis=0)
    split_at = [int(v) for v in np.cumsum(np.array(IN_SPLIT))[:-1]]
    cs = jax.nn.silu(c)
    for l in range(DEPTH):
        mod = cs @ w_ada[l] + b_ada[l]
        sh1, sc1, g1, sh2, sc2, g2 = jnp.split(mod, 6, axis=-1)
        h = rmsnorm(x, norm1_g[l]) * (1.0 + sc1[:, None]) + sh1[:, None]
        proj = h @ w_in[l]
        hq, hfp, hi, hg, aq, ak, av, iq, ik, iw, ga, gb = jnp.split(proj, split_at, axis=-1)
        ya = hgrn2_mix(hq, hfp, hi, hg, lb_all[l], hg_onorm_g[l])
        q = rmsnorm(aq.reshape(B, S, ATT_HEADS, ATT_HEAD_DIM), q_norm_g[l])
        k = rmsnorm(ak.reshape(B, S, ATT_GROUPS, ATT_HEAD_DIM), k_norm_g[l])
        v = av.reshape(B, S, ATT_GROUPS, ATT_HEAD_DIM)
        yb = dsa_mix(q, k, v, iq.reshape(B, S, IDX_HEADS, IDX_DIM), ik, iw)
        merged = jax.nn.sigmoid(ga) * (ya @ w_a[l]) + jax.nn.sigmoid(gb) * (yb @ w_b[l])
        x = x + g1[:, None] * (merged @ w_out[l])
        h2 = rmsnorm(x, norm2_g[l]) * (1.0 + sc2[:, None]) + sh2[:, None]
        x = x + g2[:, None] * peer_ffn(h2, peer_wq[l], peer_subkeys[l], peer_u[l], peer_v[l])
    return x


_drawn_inputs = setup_inputs


def setup_inputs(seed=0):
    import zlib

    import numpy as np

    out = dict(_drawn_inputs(seed))
    spreads = {}
    factors = {'norm1_g': 3.22,
     'hg_lb': 8.0,
     'hg_onorm_g': 18.108,
     'q_norm_g': 26.285,
     'k_norm_g': 25.232,
     'norm2_g': 7.526}
    for name, (base, spread) in spreads.items():
        noise = np.random.default_rng([zlib.crc32(name.encode()), seed]).standard_normal(out[name].shape)
        drawn = base * np.exp(spread * noise) if base else spread * noise
        out[name] = __import__('jax').numpy.asarray(drawn.astype(out[name].dtype))
    for name, factor in factors.items():
        out[name] = (out[name] * factor).astype(out[name].dtype)
    return out
```

```python
import concourse.bass as bass
from concourse import mybir
from contextlib import ExitStack


def hybrid_hgrn2_dsa_peer_kernel(
    nc, x, c, w_ada, b_ada, norm1_g, norm2_g, w_in, hg_lb, hg_onorm_g, q_norm_g, k_norm_g,
    w_a, w_b, w_out, peer_wq, peer_subkeys, peer_u, peer_v, out,
):
    fp32 = mybir.dt.float32
    u32 = mybir.dt.uint32
    ALU = mybir.AluOpType
    ACT = mybir.ActivationFunctionType
    AX = mybir.AxisListType

    P = 128
    D = x.shape[2]
    SEQ = x.shape[1]
    NB = SEQ // P
    KD = D // P
    HH, DK, CH = 4, 128, 64
    HGW = HH * DK
    NCH = SEQ // CH
    AH, AG, HD = 8, 2, 64
    AR = AH // AG
    IH = 8
    TOPK = min(256, SEQ // 4)
    PH, PK = 8, 16
    NKEYS = peer_subkeys.shape[3]
    EPS = 1e-6
    IDX_SCALE = (64 ** -0.5) * (IH ** -0.5)
    ATT_SCALE = HD ** -0.5
    TAKEN = -3.0e38
    FUTURE = -1.0e38
    BARRED = -1.0e35
    NW = 2
    RING = 16
    O_Q, O_F, O_I, O_G = 0, HGW, 2 * HGW, 3 * HGW
    O_AQ = 4 * HGW
    O_IQ = O_AQ + AH * HD + 2 * AG * HD
    O_IK = O_IQ + IH * HD
    O_IW = O_IK + HD
    O_GA = O_IW + IH
    O_GB = O_GA + D

    QUARTERS = [(s0, (s0 // CH + 1) * CH) for s0 in range(0, P, CH // 2)]

    fills, reader = {}, []

    def plan(key, engine):
        fills[key] = len(reader)
        reader.append(engine)

    for n in range(2):
        for h in range(2):
            plan(("ada", n, h), "V")
    for b in range(NB):
        for h in range(2):
            plan(("hT", b, h), "A")
    for j in range(8):
        plan(("qf", j), "A")
    for b in range(NB):
        for h in range(2):
            plan(("ig", b, h), "A")
    for b in range(NB):
        for h in range(2):
            plan(("att_in", b, h), "A")
    for j in range(5):
        plan(("idx_in", j), "A")
    plan(("iw",), "V")
    for n in range(2, 6):
        for h in range(2):
            plan(("ada", n, h), "V")
    for b in range(NB):
        plan(("intra", b), "A")
        plan(("kl", b), "A")
        plan(("dS", 2 * b), "V")
        plan(("dS", 2 * b + 1), "V")
        plan(("o", b), "A")
    plan(("kT",), "A")
    for b in range(NB):
        plan(("qT", b), "A")
    for b in range(NB):
        if b:
            for h in range(IH):
                plan(("I", b, h), "A")
        plan(("S", b, 0), "V")
        for h in range(AH):
            if h + 1 < AH:
                plan(("S", b, h + 1), "V")
            plan(("pT", b, h), "A")
            plan(("yb", b, h), "V")
    for b in range(NB):
        plan(("yaT", b), "A")
        plan(("ybT", b), "A")
    for w in ("ga", "gb"):
        for b in range(NB):
            for h in range(2):
                plan((w, b, h), "A")
    for w in ("ya_wa", "yb_wb"):
        for b in range(NB):
            for h in range(2):
                plan((w, b, h), "V")
    for b in range(NB):
        for h in range(2):
            plan(("mT", b, h), "A")
    for b in range(NB):
        for h in range(2):
            plan(("out", b, h), "V")
    for b in range(NB):
        for h in range(2):
            plan(("h2T", b, h), "A")
    for j in range(4):
        plan(("sk", j), "A")
    plan(("qry", 0), "A")
    for j in range(16):
        if j + 1 < 16:
            plan(("qry", j + 1), "A")
        plan(("sc", j), "A")

    def read_by_then(k, engine):
        return sum(e == engine for e in reader[: k + 1])

    ctx = ExitStack()
    with ctx:
        def sb(name, n, dt=fp32, parts=P):
            return ctx.enter_context(nc.sbuf_tensor(name, [parts, n], dt))

        def sem(name):
            return ctx.enter_context(nc.semaphore(name))

        PS = ctx.enter_context(nc.psum_tensor("PS", [P, 8, 512], fp32))

        XR = sb("XR", 4096)
        MODS = sb("MODS", 6144)
        WR = sb("WR", 16384)
        HT = sb("HT", 4096)
        FQ = sb("FQ", 4096)
        VG = sb("VG", 4096)
        AI = sb("AI", 5632)
        T1 = sb("T1", 2048)
        T2 = sb("T2", 2048)
        SM = sb("SM", 2048)
        ident = sb("ident", 128)
        tri = sb("tri", 512)
        dist0 = sb("dist0", 512)
        st = sb("st", 256)
        cs = sb("cs", 32)
        lbt = sb("lbt", 48)
        iw = sb("iw", NB * IH)
        gqk = sb("gqk", 2 * HD)
        selw = sb("selw", 64)
        ei = sb("ei", 256, u32)
        gates = sb("gates", 256)
        idx_now = sb("idx_now", 32, u32)
        aw = sb("aw", 64)
        io16 = sb("io16", 16)

        def v3(t, a, b, off=0):
            return t[:, off:off + a * b].rearrange("p (a b) -> p a b", a=a)

        xt = v3(XR, NB, D)
        mods = v3(MODS, 6, D)
        hT = v3(HT, KD, SEQ)
        hq_f, hq_q = v3(FQ, HH, SEQ, 2048), v3(FQ, HH, SEQ)
        vi, gi = v3(VG, NB, HGW), v3(VG, NB, HGW, 2048)
        aq = v3(AI, NB, AH * HD)
        akv = v3(AI, NB, 2 * AG * HD, 2048)
        iqT = v3(AI, 4, SEQ, 3072)
        ikT = AI[:, 5120:5632]
        t1, t2 = v3(T1, HH, SEQ), v3(T2, HH, SEQ)
        t3, t4 = v3(XR, HH, SEQ), v3(XR, HH, SEQ, 2048)
        klT, inT = v3(SM, HH, DK), v3(SM, HH, P, 512)
        state = SM[:, 1024:2048].rearrange("p (v h e) -> p v h e", v=2, h=HH)
        ya = v3(MODS, NB, HGW)
        yb = v3(SM, NB, AH * HD)
        hbuf = v3(VG, 2, D)
        normg = T1[:, 0:D]
        junk = T1[:, D:2 * D]
        qn = T1[:, :].rearrange("p (b r g d) -> p b r g d", b=NB, r=AR, g=AG)
        qT = v3(FQ, NB * AR, P)
        kT = FQ[:, 2048:2560]
        kn = v3(FQ, NB, P, 2560)
        onorm = gates[:, 0:HD * 2]
        scratch = v3(dist0, HH, DK)
        I_t, wk, dm = VG[:, 0:512], VG[:, 512:1024], VG[:, 1024:1536]
        rl = v3(VG, 2, 512, 1536)
        zz = v3(VG, 2, 512, 2560)
        pp = v3(T2, 2, 512)
        pT = T2[:, 1024:2048].rearrange("p (v s t) -> p v s t", v=2, s=NB)
        m1, m2 = v3(FQ, NB, D), v3(VG, NB, D)
        yaT, ybT = v3(T1, 4, SEQ), v3(T2, 4, SEQ)
        mT = hT
        h2 = v3(FQ, NB, D)
        h2T = v3(VG, KD, SEQ)
        ot = v3(AI, 2, 512, 2048)
        skn, skT = v3(T2, 16, P), v3(SM, 16, P)
        qyT = v3(T1, 2, SEQ)
        norm2 = T1[:, 1024:2048]
        cand, onehot = VG[:, 0:2048], VG[:, 2048:4096]
        acc, unread = v3(MODS, 2, D), v3(SM, 2, D)

        def scores(b):
            return v3(HT, 16, NKEYS, 2048 * b) if b < 2 else v3(AI, 16, NKEYS, 2048 * (b - 2))

        w_ring = [v3(WR, KD, D, 8192 * s) for s in range(NW)]
        rows = v3(WR, RING, D)

        filled = sem("filled")
        act_read = sem("act_read")
        dve_read = sem("dve_read")
        w_loaded = [sem(f"w_loaded{s}") for s in range(NW)]
        small_in = sem("small_in")
        x_in = sem("x_in")
        x_again = sem("x_again")
        norm2_in = sem("norm2_in")
        sk_in = sem("sk_in")
        ikd = sem("ikd")
        const = sem("const")
        v_step = sem("v_step")
        a_step = sem("a_step")
        c_exp = sem("c_exp")
        cs_ready = sem("cs_ready")
        ms_v, ms_a = sem("ms_v"), sem("ms_a")
        h_ready = sem("h_ready")
        hg_v, hg_a = sem("hg_v"), sem("hg_a")
        masked = sem("masked")
        state_zero = sem("state_zero")
        weights_set = sem("weights_set")
        q_ready = sem("q_ready")
        i_masked = sem("i_masked")
        d_ready, d_masked = sem("d_ready"), sem("d_masked")
        relu_ready, relu_used = sem("relu_ready"), sem("relu_used")
        z_ready, p_ready = sem("z_ready"), sem("p_ready")
        yb_ready = sem("yb_ready")
        m_ready = sem("m_ready")
        x_ready = sem("x_ready")
        h2_ready = sem("h2_ready")
        route_e, route_x = sem("route_e"), sem("route_x")
        routed = sem("routed")
        idx_set = sem("idx_set")
        row_in = [sem(f"row_in{s}") for s in range(RING)]
        row_used = sem("row_used")
        slot_free = sem("slot_free")
        gelu_ready = sem("gelu_ready")
        y_ready = sem("y_ready")
        out_done = sem("out_done")

        block = ctx.enter_context(nc.Block())

        tiles = []
        wt = {}

        def tile(name, src, chunks=KD):
            wt[name] = len(tiles)
            tiles.append((name, src, chunks))

        wav = w_ada[0].rearrange("(k p) n -> p k n", p=P)
        wiv = w_in[0].rearrange("(k p) n -> p k n", p=P)
        for n in range(2):
            tile(f"ada{n}", wav[:, :, n * D:(n + 1) * D])
        tile("qf", wiv[:, :, O_Q:O_I])
        tile("ig", wiv[:, :, O_I:O_AQ])
        tile("att", wiv[:, :, O_AQ:O_IQ])
        tile("idx", None)
        for n in range(2, 6):
            tile(f"ada{n}", wav[:, :, n * D:(n + 1) * D])
        tile("ga", wiv[:, :, O_GA:O_GB])
        tile("gb", wiv[:, :, O_GB:O_GB + D])
        tile("wab", None)
        tile("wout", w_out[0].rearrange("(k p) n -> p k n", p=P))
        wqv = peer_wq[0].rearrange("(k p) n -> p k n", p=P)
        tile("wq0", wqv[:, :, 0:D])
        tile("wq1", wqv[:, :, D:2 * D])
        parts_of = {"idx": 4, "wab": 2}
        last_fill = {"qf": ("qf", 7), "ig": ("ig", NB - 1, 1), "att": ("att_in", NB - 1, 1), "idx": ("iw",),
                     "ga": ("ga", NB - 1, 1), "gb": ("gb", NB - 1, 1), "wab": ("yb_wb", NB - 1, 1),
                     "wout": ("out", NB - 1, 1), "wq0": ("qry", 7), "wq1": ("qry", 15)}
        for n in range(6):
            last_fill[f"ada{n}"] = ("ada", n, 1)

        def tile_loaded(eng, name):
            i = wt[name]
            n = sum(16 * parts_of.get(tiles[j][0], 1) for j in range(i % NW, i + 1, NW))
            eng.wait_ge(w_loaded[i % NW], n)
            return w_ring[i % NW]

        def fill_read(eng, key):
            k = fills[key]
            who = reader[k]
            eng.wait_ge(act_read if who == "A" else dve_read, read_by_then(k, who))

        @block.sync
        def _(sp):
            with nc.allow_non_contiguous_dma(reason="small columns"):
                sp.dma_start(cs[:, 0:KD], c[0].rearrange("(k p) -> p k", p=P)).then_inc(small_in, 16)
                sp.dma_start(lbt[:, 0:8].rearrange("p (l h) -> p l h", l=2),
                             hg_lb.rearrange("l (h p) -> p l h", p=P)).then_inc(small_in, 16)
            sp.dma_start(MODS[:, :], b_ada[0:1, :].to_broadcast([P, 6 * D])).then_inc(small_in, 16)
            sp.dma_start(normg, norm1_g[0:1, :].to_broadcast([P, D])).then_inc(small_in, 16)
            sp.dma_start(gqk[:, 0:HD], q_norm_g[0:1, :].to_broadcast([P, HD])).then_inc(small_in, 16)
            sp.dma_start(gqk[:, HD:2 * HD], k_norm_g[0:1, :].to_broadcast([P, HD])).then_inc(small_in, 16)
            sp.dma_start(onorm, hg_onorm_g[0:1, :].to_broadcast([P, DK])).then_inc(small_in, 16)
            sp.dma_start(xt, x[0].rearrange("(b p) d -> p b d", p=P)).then_inc(x_in, 16)
            for i, (name, src, chunks) in enumerate(tiles):
                if i >= NW:
                    sp.wait_ge(filled, fills[last_fill[tiles[i - NW][0]]] + 1)
                slot, s = w_ring[i % NW], w_loaded[i % NW]
                if name == "idx":
                    n = IH * HD
                    sp.dma_start(slot[:, :, 0:n], wiv[:, :, O_IQ:O_IK]).then_inc(s, 16)
                    sp.dma_start(slot[:, :, n:n + HD], wiv[:, :, O_IK:O_IW]).then_inc(s, 16)
                    sp.dma_start(slot[:, :, n + HD:n + 2 * HD], wiv[:, :, O_IK:O_IW]).then_inc(s, 16)
                    sp.dma_start(slot[:, :, n + 2 * HD:n + 2 * HD + IH], wiv[:, :, O_IW:O_GA]).then_inc(s, 16)
                elif name == "wab":
                    sp.dma_start(slot[:, 0:4, :], w_a[0].rearrange("(k p) n -> p k n", p=P)).then_inc(s, 16)
                    sp.dma_start(slot[:, 4:8, :], w_b[0].rearrange("(k p) n -> p k n", p=P)).then_inc(s, 16)
                else:
                    sp.dma_start(slot[:, :, 0:src.shape[2]], src).then_inc(s, 16)
                if name == "ada5":
                    sp.wait_ge(filled, fills[("o", NB - 1)] + 1)
                    sp.dma_start(xt, x[0].rearrange("(b p) d -> p b d", p=P)).then_inc(x_again, 16)
                if name == "wout":
                    sp.wait_ge(filled, fills[("yb_wb", NB - 1, 1)] + 1)
                    sp.dma_start(norm2, norm2_g[0:1, :].to_broadcast([P, D])).then_inc(norm2_in, 16)
                    sp.dma_start(skn, peer_subkeys[0].rearrange("h s n d -> n (h s) d")).then_inc(sk_in, 16)
            for b in range(NB):
                sp.wait_ge(y_ready, b + 1)
                sp.dma_start(out[0, b * P:(b + 1) * P, :], xt[:, b, :]).then_inc(out_done, 16)
            sp.wait_ge(out_done, 16 * NB)

        @block.gpsimd
        def _(pool):
            pool.memset(ident[:, :], 0.0).then_inc(const, 1)
            pool.wait_ge(const, 1)
            pool.affine_select(out=ident[:, :], in_=ident[:, :], compare_op=ALU.not_equal, fill=1.0,
                               base=0, pattern=[[-1, P]], channel_multiplier=1).then_inc(const, 1)
            pool.memset(tri[:, :], 1.0).then_inc(const, 1)
            pool.wait_ge(const, 3)
            pool.memset(tri[:, 0:SEQ:CH], 0.0).then_inc(const, 1)
            pool.memset(inT, 0.0).then_inc(const, 1)
            pool.iota(io16[:, :], pattern=[[1, PK]], base=0, channel_multiplier=0,
                      allow_small_or_imprecise_dtypes=True).then_inc(const, 1)
            for b in range(NB):
                fill_read(pool, ("intra", b))
                pool.affine_select(out=inT, in_=inT, compare_op=ALU.is_ge, fill=0.0, base=0,
                                   pattern=[[0, HH], [1, P]], channel_multiplier=-1).then_inc(masked, 1)
            fill_read(pool, ("dS", NCH - 1))
            pool.iota(dist0[:, :], pattern=[[1, SEQ]], base=0, channel_multiplier=-1,
                      allow_small_or_imprecise_dtypes=True).then_inc(const, 1)
            for b in range(NB):
                if b:
                    pool.wait_ge(relu_used, IH * b)
                    last = I_t[:, b * P:(b + 1) * P]
                    pool.affine_select(out=last, in_=last, compare_op=ALU.is_ge, fill=FUTURE, base=0,
                                       pattern=[[-1, P]], channel_multiplier=1).then_inc(i_masked, 1)
                else:
                    pool.wait_ge(d_ready, 1)
                    pool.affine_select(out=dm[:, 0:P], in_=dm[:, 0:P], compare_op=ALU.is_ge, fill=BARRED,
                                       base=0, pattern=[[-1, P]], channel_multiplier=1).then_inc(d_masked, 1)
            for b in range(NB):
                pool.wait_ge(routed, b + 1)
                with pool.Fori(0, PH // 2) as i:
                    for u in range(2):
                        head = 2 * i + (u + PH * b)
                        now = idx_now[:, u * PK:(u + 1) * PK]
                        pool.tensor_copy(now, ei[:, bass.ds((2 * i + u) * PK + (b % 2) * P, PK)]).then_inc(idx_set, 1)
                        pool.wait_ge(idx_set, head + 1)
                        pool.sem_inc(slot_free, 1)
                        for tab, src in enumerate((peer_u, peer_v)):
                            for k in range(PK):
                                pool.wait_ge(row_used, 2 * PK * head + tab * PK + k + 1)
                                pool.sem_inc(slot_free, 1)
                                pool.indirect_dma_start(
                                    rows[:, k, :], None, src[0],
                                    bass.IndirectOffsetOnAxis(ap=now[:, k:k + 1], axis=0)).then_inc(row_in[k], 16)

        @block.scalar
        def _(act):
            chain = [0]

            def step(ins):
                chain[0] += 1
                ins.then_inc(a_step, 1)
                act.wait_ge(a_step, chain[0])

            def take(key, out_ap, in_ap):
                k = fills[key]
                act.wait_ge(filled, k + 1)
                nc.scalar.activation(out_ap, in_ap(PS[:, k % 8, :]), ACT.Copy).then_inc(act_read, 1)

            whole = lambda ps: ps
            quads = lambda ps: ps.rearrange("p (a b) -> p a b", a=4)
            act.wait_ge(small_in, 112)
            nc.scalar.activation(cs[:, KD:2 * KD], cs[:, 0:KD], ACT.Exp, scale=-1.0).then_inc(c_exp, 1)
            act.wait_ge(cs_ready, 1)
            nc.scalar.activation(lbt[:, 8:16], lbt[:, 16:24], ACT.Exp).then_inc(c_exp, 1)
            act.wait_ge(x_in, 16)
            for b in range(NB):
                step(nc.scalar.activation(junk, xt[:, b, :], ACT.Square, accum_out=st[:, b:b + 1]))
            nc.scalar.activation(junk[:, 0:1], st[:, 0:1], ACT.Copy).then_inc(ms_a, 1)
            act.wait_ge(ms_v, 1)
            nc.scalar.activation(st[:, 8:12], st[:, 4:8], ACT.Sqrt).then_inc(ms_a, 1)
            for b in range(NB):
                for h in range(2):
                    take(("hT", b, h), hT[:, 4 * h:4 * h + 4, b * P:(b + 1) * P], quads)
            for j in range(8):
                take(("qf", j), hq_q[:, j, :] if j < 4 else hq_f[:, j - 4, :], whole)
            fill_read(act, ("qf", 7))
            act.wait_ge(hg_v, 1)
            step(nc.scalar.activation(hq_f, hq_f, ACT.Exp, scale=-1.0))
            nc.scalar.activation(t1, hq_q, ACT.Exp, scale=-1.0).then_inc(hg_a, 1)
            for b in range(NB):
                for h in range(2):
                    take(("ig", b, h), (vi, gi)[h][:, b, :], whole)
            act.wait_ge(hg_v, 2)
            nc.scalar.activation(t1, hq_f, ACT.Ln).then_inc(hg_a, 1)
            for b in range(NB):
                take(("att_in", b, 0), aq[:, b, :], whole)
                take(("att_in", b, 1), akv[:, b, :], lambda ps: ps[:, 0:256])
            act.wait_ge(hg_v, 3)
            step(nc.scalar.activation(t3, t1, ACT.Exp))
            step(nc.scalar.activation(t4, t2, ACT.Exp))
            nc.scalar.activation(t1, t1, ACT.Exp, scale=-1.0).then_inc(hg_a, 1)
            act.wait_ge(hg_v, 4)
            step(nc.scalar.activation(lbt[:, 16:48], st[:, 128:160], ACT.Exp))
            nc.scalar.activation(t2, t2, ACT.Exp).then_inc(hg_a, 1)
            for j in range(5):
                take(("idx_in", j), iqT[:, j, :] if j < 4 else ikT, whole)
            for b in range(NB):
                if b:
                    act.wait_ge(filled, fills[("o", b - 1)] + 1)
                k = fills[("intra", b)]
                act.wait_ge(filled, k + 1)
                if b == 0:
                    act.wait_ge(const, 6)
                for s0, c1 in QUARTERS:
                    ins = nc.scalar.activation(inT[s0:s0 + CH // 2, :, s0:c1],
                                               quads(PS[s0:s0 + CH // 2, k % 8, :])[:, :, s0:c1], ACT.Copy)
                ins.then_inc(act_read, 1)
                take(("kl", b), klT, quads)
                take(("o", b), ya[:, b, :], whole)
            fill_read(act, ("o", NB - 1))
            act.wait_ge(hg_v, 7)
            step(nc.scalar.activation(t1, gi, ACT.Exp, scale=-1.0))
            nc.scalar.activation(t2, ya, ACT.Square).then_inc(hg_a, 1)
            act.wait_ge(hg_v, 8)
            nc.scalar.activation(t2, aq, ACT.Square).then_inc(hg_a, 1)
            act.wait_ge(hg_v, 9)
            nc.scalar.activation(t2[:, :, 0:P], akv[:, :, 0:P], ACT.Square).then_inc(hg_a, 1)
            act.wait_ge(hg_v, 10)
            nc.scalar.activation(st[:, 128:184], st[:, 64:120], ACT.Sqrt).then_inc(hg_a, 1)
            act.wait_ge(q_ready, 1)
            take(("kT",), kT, whole)
            for b in range(NB):
                take(("qT", b), qT[:, 4 * b:4 * b + 4, :], quads)
            nI = 0
            n = 0

            def exp_row(b, h, n):
                W = (b + 1) * P
                act.wait_ge(z_ready, n + 1)
                if n >= 2:
                    act.wait_ge(filled, fills[("pT", (n - 2) // AH, (n - 2) % AH)] + 1)
                nc.scalar.activation(pp[:, n % 2, 0:W], zz[:, n % 2, 0:W], ACT.Exp,
                                     bias=st[:, 16 + n:17 + n], accum_out=st[:, 64 + n:65 + n]).then_inc(p_ready, 1)

            for b in range(NB):
                W = (b + 1) * P
                if b:
                    for h in range(IH):
                        k = fills[("I", b, h)]
                        act.wait_ge(filled, k + 1)
                        if nI >= 2:
                            act.wait_ge(relu_used, nI - 1)
                        nc.scalar.activation(rl[:, nI % 2, 0:W], PS[:, k % 8, 0:W], ACT.Relu).then_inc(act_read, 1)
                        nI += 1
                for h in range(AH):
                    exp_row(b, h, n)
                    if n >= 2:
                        act.wait_ge(filled, fills[("yb", (n - 2) // AH, (n - 2) % AH)] + 1)
                    take(("pT", b, h), pT[:, n % 2, 0:b + 1, :],
                         lambda ps: ps[:, 0:W].rearrange("p (a b) -> p a b", a=W // P))
                    n += 1
            for b in range(NB):
                if b == 0:
                    act.wait_ge(filled, fills[("yb", NB - 1, AH - 1)] + 1)
                take(("yaT", b), yaT[:, :, b * P:(b + 1) * P], quads)
                take(("ybT", b), ybT[:, :, b * P:(b + 1) * P], quads)
            for w, m in (("ga", m1), ("gb", m2)):
                act.wait_ge(yb_ready, 1)
                for b in range(NB):
                    for h in range(2):
                        k = fills[(w, b, h)]
                        act.wait_ge(filled, k + 1)
                        nc.scalar.activation(m[:, b, 512 * h:512 * h + 512], PS[:, k % 8, :], ACT.Exp,
                                             scale=-1.0).then_inc(act_read, 1)
            for b in range(NB):
                for h in range(2):
                    if b == 0 and h == 0:
                        act.wait_ge(filled, fills[("gb", NB - 1, 1)] + 1)
                    take(("mT", b, h), mT[:, 4 * h:4 * h + 4, b * P:(b + 1) * P], quads)
            for b in range(NB):
                act.wait_ge(x_ready, b + 1)
                step(nc.scalar.activation(T1[:, 0:D], xt[:, b, :], ACT.Square, accum_out=st[:, b:b + 1]))
            nc.scalar.activation(T1[:, 0:1], st[:, 0:1], ACT.Copy).then_inc(ms_a, 1)
            act.wait_ge(ms_v, 2)
            nc.scalar.activation(st[:, 8:12], st[:, 4:8], ACT.Sqrt).then_inc(ms_a, 1)
            for b in range(NB):
                for h in range(2):
                    take(("h2T", b, h), h2T[:, 4 * h:4 * h + 4, b * P:(b + 1) * P], quads)
            for j in range(4):
                take(("sk", j), skT[:, 4 * j:4 * j + 4, :], quads)

            def take_q(j):
                if j == 0:
                    act.wait_ge(h2_ready, NB)
                if j >= 2:
                    act.wait_ge(filled, fills[("sc", j - 2)] + 1)
                take(("qry", j), qyT[:, j % 2, :], whole)

            take_q(0)
            for j in range(16):
                if j + 1 < 16:
                    take_q(j + 1)
                k = fills[("sc", j)]
                act.wait_ge(filled, k + 1)
                ps = quads(PS[:, k % 8, :])
                step(nc.scalar.activation(HT[:, :].rearrange("p (b j n) -> p b j n", b=2, j=16)[:, :, j, :],
                                          ps[:, 0:2, :], ACT.Copy))
                nc.scalar.activation(AI[:, 0:4096].rearrange("p (b j n) -> p b j n", b=2, j=16)[:, :, j, :],
                                     ps[:, 2:4, :], ACT.Copy).then_inc(act_read, 1)
            def gates_exp(b):
                half = gates[:, (b % 2) * P:(b % 2) * P + P]
                act.wait_ge(route_e, b + 1)
                nc.scalar.activation(half, half, ACT.Exp).then_inc(route_x, 1)

            gates_exp(0)
            for b in range(NB):
                if b + 1 < NB:
                    gates_exp(b + 1)
                with act.Fori(0, PH) as i:
                    act.wait_ge(row_used, i * (2 * PK) + (RING + PK + 2 * PK * PH * b))
                    nc.scalar.activation(aw[:, PK:2 * PK], aw[:, 0:PK], ACT.Gelu).then_inc(gelu_ready, 1)

        @block.tensor
        def _(pe):
            def bank(key):
                k = fills[key]
                if k >= 8:
                    who = reader[k - 8]
                    pe.wait_ge(act_read if who == "A" else dve_read, read_by_then(k - 8, who))
                return PS[:, k % 8, :]

            def done(ins):
                ins.then_inc(filled, 1)

            def product(key, parts, n=512, ps=None):
                ps = bank(key) if ps is None else ps
                for i, (lhsT, rhs) in enumerate(parts):
                    ins = nc.tensor.matmul(ps[:, 0:n], lhsT, rhs, start=i == 0, stop=i == len(parts) - 1)
                return ins

            def turned(key, ins_):
                ps = bank(key)
                for i, a in enumerate(ins_):
                    last = nc.tensor.transpose(ps[:, i * P:(i + 1) * P], a, ident[:, :])
                done(last)

            pe.wait_ge(const, 2)
            pe.wait_ge(cs_ready, 2)

            def ada(n):
                w = tile_loaded(pe, f"ada{n}")
                for h in range(2):
                    done(product(("ada", n, h), [(cs[:, KD + k:KD + k + 1].broadcast_to([P, P]), w[:, k, 512 * h:512 * h + 512]) for k in range(KD)]))

            def token_major(key, w, src, halves, chunks=KD, k0=0):
                for b in range(NB):
                    for h, n in enumerate(halves):
                        done(product((key, b, h), [(src[:, k, b * P:(b + 1) * P], w[:, k0 + k, 512 * h:512 * h + n])
                                                   for k in range(chunks)], n))

            ada(0)
            ada(1)
            for b in range(NB):
                pe.wait_ge(h_ready, b + 1)
                for h in range(2):
                    turned(("hT", b, h), [hbuf[:, b % 2, (4 * h + i) * P:(4 * h + i + 1) * P] for i in range(4)])
            w = tile_loaded(pe, "qf")
            fill_read(pe, ("hT", NB - 1, 1))
            for j in range(8):
                done(product(("qf", j), [(w[:, k, j * P:(j + 1) * P], hT[:, k, :]) for k in range(KD)]))
            token_major("ig", tile_loaded(pe, "ig"), hT, (512, 512))
            token_major("att_in", tile_loaded(pe, "att"), hT, (512, 256))
            w = tile_loaded(pe, "idx")
            for j in range(5):
                done(product(("idx_in", j), [(w[:, k, j * P:(j + 1) * P], hT[:, k, :]) for k in range(KD)]))
            ps = bank(("iw",))
            for b in range(NB):
                last = product(None, [(hT[:, k, b * P:(b + 1) * P], w[:, k, 5 * P:5 * P + IH]) for k in range(KD)],
                               IH, ps[:, b * IH:(b + 1) * IH])
            done(last)
            for n in range(2, 6):
                ada(n)
            pe.wait_ge(hg_v, 7)
            fill_read(pe, ("ig", NB - 1, 1))
            for b in range(NB):
                t = slice(b * P, (b + 1) * P)
                ps = bank(("intra", b))
                for h in range(HH):
                    for s0, c1 in QUARTERS:
                        last = nc.tensor.matmul(ps[s0:s0 + CH // 2, h * P + s0:h * P + c1],
                                                t1[:, h, b * P + s0:b * P + s0 + CH // 2],
                                                t3[:, h, b * P + s0:b * P + c1], start=True, stop=True)
                done(last)
                turned(("kl", b), [t2[:, h, t] for h in range(HH)])
                fill_read(pe, ("kl", b))
                for j in range(2):
                    ps = bank(("dS", 2 * b + j))
                    s = slice(j * CH, (j + 1) * CH)
                    for h in range(HH):
                        e = slice(h * DK, (h + 1) * DK)
                        last = nc.tensor.matmul(ps[:, e], klT[s, h, :], vi[s, b, e], start=True, stop=True)
                    done(last)
                pe.wait_ge(masked, b + 1)
                pe.wait_ge(state_zero, 1)
                fill_read(pe, ("dS", 2 * b))
                ps = bank(("o", b))
                for h in range(HH):
                    e = slice(h * DK, (h + 1) * DK)
                    nc.tensor.matmul(ps[:, e], inT[:, h, :], vi[:, b, e], start=True, stop=False)
                    nc.tensor.matmul(ps[:, e], hq_q[:, h, t], state[:, 0, h, :], start=False, stop=False)
                    last = nc.tensor.matmul(ps[:, e], t4[:, h, t], state[:, 1, h, :], start=False, stop=True)
                done(last)
            pe.wait_ge(q_ready, 1)
            turned(("kT",), [kn[:, b, :] for b in range(NB)])
            for b in range(NB):
                turned(("qT", b), [qn[:, b, r, :, :] for r in range(AR)])
            fill_read(pe, ("qT", NB - 1))

            def att_scores(b, h):
                g, r = h // AR, h % AR
                q = qT[g * HD:(g + 1) * HD, b * AR + r, :]
                done(product(("S", b, h), [(q, kT[g * HD:(g + 1) * HD, 0:(b + 1) * P])], (b + 1) * P))

            n = 0
            for b in range(NB):
                if b:
                    for h in range(IH):
                        s = slice((h % 2) * HD, (h % 2 + 1) * HD)
                        done(product(("I", b, h), [(iqT[s, h // 2, b * P:(b + 1) * P], ikT[s, 0:(b + 1) * P])],
                                     (b + 1) * P))
                att_scores(b, 0)
                for h in range(AH):
                    if h + 1 < AH:
                        att_scores(b, h + 1)
                    pe.wait_ge(p_ready, n + 1)
                    turned(("pT", b, h), [pp[:, n % 2, i * P:(i + 1) * P] for i in range(b + 1)])
                    fill_read(pe, ("pT", b, h))
                    g = h // AR
                    done(product(("yb", b, h), [(pT[:, n % 2, i, :], akv[:, i, P + g * HD:P + (g + 1) * HD])
                                                for i in range(b + 1)], HD))
                    n += 1
            pe.wait_ge(yb_ready, 1)
            for b in range(NB):
                turned(("yaT", b), [ya[:, b, i * P:(i + 1) * P] for i in range(4)])
                turned(("ybT", b), [yb[:, b, i * P:(i + 1) * P] for i in range(4)])
            token_major("ga", tile_loaded(pe, "ga"), hT, (512, 512))
            token_major("gb", tile_loaded(pe, "gb"), hT, (512, 512))
            w = tile_loaded(pe, "wab")
            fill_read(pe, ("ybT", NB - 1))
            token_major("ya_wa", w, yaT, (512, 512), 4, 0)
            token_major("yb_wb", w, ybT, (512, 512), 4, 4)
            for b in range(NB):
                for h in range(2):
                    pe.wait_ge(m_ready, 2 * b + h + 1)
                    turned(("mT", b, h), [m1[:, b, (4 * h + i) * P:(4 * h + i + 1) * P] for i in range(4)])
            w = tile_loaded(pe, "wout")
            fill_read(pe, ("mT", NB - 1, 1))
            token_major("out", w, mT, (512, 512))
            for b in range(NB):
                pe.wait_ge(h2_ready, b + 1)
                for h in range(2):
                    turned(("h2T", b, h), [h2[:, b, (4 * h + i) * P:(4 * h + i + 1) * P] for i in range(4)])
            pe.wait_ge(sk_in, 16)
            for j in range(4):
                turned(("sk", j), [skn[:, 4 * j + i, :] for i in range(4)])
            fill_read(pe, ("sk", 3))

            def query(j):
                w = tile_loaded(pe, f"wq{j // 8}")
                done(product(("qry", j), [(w[:, k, (j % 8) * P:(j % 8 + 1) * P], h2T[:, k, :]) for k in range(KD)]))

            query(0)
            for j in range(16):
                if j + 1 < 16:
                    query(j + 1)
                fill_read(pe, ("qry", j))
                ps = bank(("sc", j))
                for b in range(NB):
                    last = nc.tensor.matmul(ps[:, b * P:(b + 1) * P], qyT[:, j % 2, b * P:(b + 1) * P], skT[:, j, :],
                                            start=True, stop=True)
                done(last)

        @block.vector
        def _(dve):
            V = nc.vector
            chain = [0]

            def step(ins):
                chain[0] += 1
                ins.then_inc(v_step, 1)
                dve.wait_ge(v_step, chain[0])

            def ready(key):
                k = fills[key]
                dve.wait_ge(filled, k + 1)
                return PS[:, k % 8, :]

            def take(ins):
                ins.then_inc(dve_read, 1)

            def one_over_one_plus(t):
                step(V.tensor_scalar(t, t, 1.0, None, ALU.add))
                step(V.reciprocal(t, t))

            def spread(t, shape):
                return t.broadcast_to(shape)

            dve.wait_ge(small_in, 112)
            step(V.tensor_tensor(lbt[:, 40:44], lbt[:, 0:4], lbt[:, 4:8], ALU.max))
            V.tensor_tensor(lbt[:, 16:24].rearrange("p (l h) -> p l h", l=2),
                            lbt[:, 0:8].rearrange("p (l h) -> p l h", l=2),
                            lbt[:, 40:44].unsqueeze(1).broadcast_to([P, 2, 4]), ALU.subtract).then_inc(cs_ready, 1)
            dve.wait_ge(c_exp, 1)
            one_over_one_plus(cs[:, KD:2 * KD])
            V.tensor_tensor(cs[:, KD:2 * KD], cs[:, KD:2 * KD], cs[:, 0:KD], ALU.mult).then_inc(cs_ready, 1)
            dve.wait_ge(c_exp, 2)
            step(V.tensor_tensor(lbt[:, 16:20], lbt[:, 8:12], lbt[:, 12:16], ALU.add))
            step(V.reciprocal(lbt[:, 16:20], lbt[:, 16:20]))
            step(V.tensor_tensor(lbt[:, 0:4], lbt[:, 8:12], lbt[:, 16:20], ALU.mult))
            step(V.tensor_scalar(lbt[:, 4:8], lbt[:, 0:4], -1.0, 1.0, ALU.mult, ALU.add))
            dve.wait_ge(ms_a, 1)
            V.tensor_scalar(st[:, 4:8], st[:, 0:4], 1.0 / D, EPS, ALU.mult, ALU.add).then_inc(ms_v, 1)
            dve.wait_ge(ms_a, 2)
            step(V.reciprocal(st[:, 12:16], st[:, 8:12]))

            def ada(n):
                for h in range(2):
                    part = mods[:, n, 512 * h:512 * h + 512]
                    take(V.tensor_tensor(part, part, ready(("ada", n, h)), ALU.add))

            ada(0)
            ada(1)
            fill_read(dve, ("ada", 1, 1))
            step(V.scalar_tensor_tensor(out=mods[:, 1, :], in0=mods[:, 1, :], scalar=1.0, in1=normg,
                                        op0=ALU.add, op1=ALU.mult))
            for b in range(NB):
                if b >= 2:
                    dve.wait_ge(filled, fills[("hT", b - 2, 1)] + 1)
                step(V.scalar_tensor_tensor(out=hbuf[:, b % 2, :], in0=xt[:, b, :], scalar=st[:, 12 + b:13 + b],
                                            in1=mods[:, 1, :], op0=ALU.mult, op1=ALU.mult))
                V.tensor_tensor(hbuf[:, b % 2, :], hbuf[:, b % 2, :], mods[:, 0, :], ALU.add).then_inc(h_ready, 1)
            dve.wait_ge(filled, fills[("ada", 1, 1)] + 1)
            dve.wait_ge(h_ready, NB)
            V.memset(st[:, 250:251], 0.0).then_inc(hg_v, 1)
            dve.wait_ge(hg_a, 1)
            one_over_one_plus(hq_f)
            for h in range(HH):
                step(V.tensor_scalar(hq_f[:, h, :], hq_f[:, h, :], lbt[:, 4 + h:5 + h], lbt[:, h:h + 1],
                                     ALU.mult, ALU.add))
            one_over_one_plus(t1)
            V.tensor_tensor(hq_q, hq_q, t1, ALU.mult).then_inc(hg_v, 1)
            dve.wait_ge(hg_a, 2)
            step(V.tensor_scalar(hq_f, hq_f, -1.0, 1.0, ALU.mult, ALU.add))
            dve.wait_ge(const, 4)
            for h in range(HH):
                step(V.tensor_tensor_scan(t2[:, h, :], tri[:, :], t1[:, h, :], 0.0, ALU.mult, ALU.add))
            chunks = lambda t: t.rearrange("p h (n c) -> p (h n) c", c=CH)
            bl = st[:, 128:160]
            bm = st[:, 96:128]
            step(V.tensor_copy(bl.unsqueeze(2), chunks(t2)[:, :, CH - 1:CH]))
            step(V.tensor_copy(bm.unsqueeze(2), chunks(t2)[:, :, CH // 2 - 1:CH // 2]))
            V.tensor_tensor(chunks(t1), chunks(t2), bm.unsqueeze(2).broadcast_to([P, HH * NCH, CH]),
                            ALU.subtract).then_inc(hg_v, 1)
            dve.wait_ge(hg_a, 3)
            V.tensor_tensor(chunks(t2), bl.unsqueeze(2).broadcast_to([P, HH * NCH, CH]), chunks(t2),
                            ALU.subtract).then_inc(hg_v, 1)
            V.tensor_tensor(t1, hq_f, t1, ALU.mult).then_inc(hg_v, 1)
            step(V.tensor_tensor(t3, hq_q, t3, ALU.mult))
            step(V.tensor_tensor(t4, hq_q, t4, ALU.mult))
            even = lambda t: t.rearrange("p h (n j c) -> p (h n) j c", j=2, c=CH)[:, :, 0, :]
            odd = lambda t: t.rearrange("p h (n j c) -> p (h n) j c", j=2, c=CH)[:, :, 1, :]
            step(V.tensor_copy(even(hq_q), even(t4)))
            step(V.memset(odd(hq_q), 0.0))
            V.memset(even(t4), 0.0).then_inc(hg_v, 1)
            dve.wait_ge(hg_a, 4)
            V.tensor_tensor(t2, hq_f, t2, ALU.mult).then_inc(hg_v, 1)
            take(V.tensor_scalar(iw[:, :], ready(("iw",))[:, 0:NB * IH], IDX_SCALE, None, ALU.mult))
            for n in range(2, 6):
                ada(n)
            V.memset(state[:, 0, :, :], 0.0).then_inc(state_zero, 1)
            dve.wait_ge(state_zero, 1)
            decay = lbt[:, 16:48].rearrange("p (h n) -> p h n", h=HH)
            for n in range(NCH):
                step(V.tensor_tensor(scratch, state[:, n % 2, :, :], decay[:, :, n:n + 1].broadcast_to([P, HH, DK]),
                                     ALU.mult))
                if n:
                    dve.wait_ge(filled, fills[("o", (n - 1) // 2)] + 1)
                take(V.tensor_tensor(state[:, (n + 1) % 2, :, :], scratch,
                                     ready(("dS", n)).rearrange("p (h e) -> p h e", h=HH), ALU.add))
                fill_read(dve, ("dS", n))
            dve.wait_ge(hg_a, 5)
            step(V.tensor_reduce(st[:, 64:80], t2.rearrange("p b (h e) -> p (b h) e", h=HH), AX.X, ALU.add))
            V.tensor_scalar(st[:, 64:80], st[:, 64:80], 1.0 / DK, EPS, ALU.mult, ALU.add).then_inc(hg_v, 1)
            one_over_one_plus(t1)
            step(V.tensor_tensor(gi, gi, t1, ALU.mult))
            g4 = gi.rearrange("p b (h e) -> p (b h) e", h=HH)
            step(V.tensor_tensor(g4, g4, onorm.unsqueeze(1).broadcast_to([P, NB * HH, DK]), ALU.mult))
            dve.wait_ge(hg_a, 6)
            step(V.tensor_reduce(st[:, 80:112], t2.rearrange("p b (h e) -> p (b h) e", h=AH), AX.X, ALU.add))
            V.tensor_scalar(st[:, 80:112], st[:, 80:112], 1.0 / HD, EPS, ALU.mult, ALU.add).then_inc(hg_v, 1)
            dve.wait_ge(hg_a, 7)
            step(V.tensor_reduce(st[:, 112:120].rearrange("p (b g) -> p b g", b=NB),
                                 t2[:, :, 0:P].rearrange("p b (g e) -> p b g e", g=AG), AX.X, ALU.add))
            V.tensor_scalar(st[:, 112:120], st[:, 112:120], 1.0 / HD, EPS, ALU.mult, ALU.add).then_inc(hg_v, 1)
            dve.wait_ge(hg_a, 8)
            step(V.reciprocal(st[:, 64:120], st[:, 128:184]))
            y4 = ya.rearrange("p b (h e) -> p (b h) e", h=HH)
            step(V.tensor_tensor(y4, y4, st[:, 64:80].unsqueeze(2).broadcast_to([P, NB * HH, DK]), ALU.mult))
            step(V.tensor_tensor(y4, y4, g4, ALU.mult))
            q4 = aq.rearrange("p b (h e) -> p (b h) e", h=AH)
            step(V.tensor_scalar(gqk[:, 0:HD], gqk[:, 0:HD], ATT_SCALE, None, ALU.mult))
            step(V.tensor_tensor(q4, q4, st[:, 80:112].unsqueeze(2).broadcast_to([P, NB * AH, HD]), ALU.mult))
            for b in range(NB):
                step(V.tensor_tensor(qn[:, b, :, :, :].rearrange("p r g d -> p g r d"),
                                     aq[:, b, :].rearrange("p (g r d) -> p g r d", g=AG, r=AR),
                                     gqk[:, 0:HD].unsqueeze(1).unsqueeze(1).broadcast_to([P, AG, AR, HD]), ALU.mult))
            k4 = akv[:, :, 0:P].rearrange("p b (g d) -> p b g d", g=AG)
            kn4 = kn.rearrange("p b (g d) -> p b g d", g=AG)
            step(V.tensor_tensor(kn4, k4, st[:, 112:120].rearrange("p (b g) -> p b g", b=NB).unsqueeze(3)
                                 .broadcast_to([P, NB, AG, HD]), ALU.mult))
            V.tensor_tensor(kn4, kn4, gqk[:, HD:2 * HD].unsqueeze(1).unsqueeze(1).broadcast_to([P, NB, AG, HD]),
                            ALU.mult).then_inc(q_ready, 1)
            def head_out(b, h, n):
                dve.wait_ge(p_ready, n + 1)
                step(V.reciprocal(st[:, 64 + n:65 + n], st[:, 64 + n:65 + n]))
                take(V.tensor_scalar(yb[:, b, h * HD:(h + 1) * HD], ready(("yb", b, h))[:, 0:HD],
                                     st[:, 64 + n:65 + n], None, ALU.mult))

            nI = n = 0
            dve.wait_ge(const, 7)
            for b in range(NB):
                W = (b + 1) * P
                if b:
                    for h in range(IH):
                        fill_read(dve, ("I", b, h))
                        weight = iw[:, b * IH + h:b * IH + h + 1]
                        if h == 0:
                            V.tensor_scalar(I_t[:, 0:W], rl[:, nI % 2, 0:W], weight, None, ALU.mult)\
                             .then_inc(relu_used, 1)
                        else:
                            V.scalar_tensor_tensor(out=I_t[:, 0:W], in0=rl[:, nI % 2, 0:W], scalar=weight,
                                                   in1=I_t[:, 0:W], op0=ALU.mult, op1=ALU.add).then_inc(relu_used, 1)
                        nI += 1
                        dve.wait_ge(relu_used, nI)
                    dve.wait_ge(i_masked, b)
                    for r in range(TOPK // 8):
                        src = I_t if r == 0 else wk
                        step(V.max(selw[:, 0:8], src[:, 0:W]))
                        step(V.match_replace(wk[:, 0:W], selw[:, 0:8], src[:, 0:W], TAKEN))
                    step(V.tensor_scalar(wk[:, 0:W], wk[:, 0:W], 0.5 * (TAKEN + FUTURE), BARRED, ALU.is_ge, ALU.mult))
                    step(V.scalar_tensor_tensor(out=dm[:, 0:W], in0=dist0[:, 0:W], scalar=float(-b * P),
                                                in1=wk[:, 0:W], op0=ALU.add, op1=ALU.add))
                else:
                    V.tensor_copy(dm[:, 0:W], dist0[:, 0:W]).then_inc(d_ready, 1)
                    dve.wait_ge(d_masked, 1)
                for h in range(AH):
                    ps = ready(("S", b, h))
                    if n >= 2:
                        dve.wait_ge(p_ready, n - 1)
                    z = zz[:, n % 2, 0:W]
                    take(V.scalar_tensor_tensor(out=z, in0=dm[:, 0:W], scalar=2.0 ** (-8.0 * (h + 1) / AH),
                                                in1=ps[:, 0:W], op0=ALU.mult, op1=ALU.add))
                    fill_read(dve, ("S", b, h))
                    V.tensor_reduce(st[:, 16 + n:17 + n], z, AX.X, ALU.max, negate=True).then_inc(z_ready, 1)
                    if h:
                        head_out(b, h - 1, n - 1)
                    n += 1
                head_out(b, AH - 1, n - 1)
            fill_read(dve, ("yb", NB - 1, AH - 1))
            V.memset(st[:, 250:251], 0.0).then_inc(yb_ready, 1)

            fill_read(dve, ("ga", NB - 1, 1))
            one_over_one_plus(FQ[:, :])
            fill_read(dve, ("gb", NB - 1, 1))
            one_over_one_plus(VG[:, :])
            for b in range(NB):
                for h in range(2):
                    part = m1[:, b, 512 * h:512 * h + 512]
                    take(V.tensor_tensor(part, part, ready(("ya_wa", b, h)), ALU.mult))
            for b in range(NB):
                for h in range(2):
                    part, other = m1[:, b, 512 * h:512 * h + 512], m2[:, b, 512 * h:512 * h + 512]
                    take(V.tensor_tensor(other, other, ready(("yb_wb", b, h)), ALU.mult))
                    fill_read(dve, ("yb_wb", b, h))
                    V.tensor_tensor(part, part, other, ALU.add).then_inc(m_ready, 1)
            dve.wait_ge(x_again, 16)
            fill_read(dve, ("ada", 5, 1))
            for b in range(NB):
                for h in range(2):
                    part = xt[:, b, 512 * h:512 * h + 512]
                    take(V.tensor_tensor(ot[:, h, :], mods[:, 2, 512 * h:512 * h + 512], ready(("out", b, h)), ALU.mult))
                    fill_read(dve, ("out", b, h))
                    ins = V.tensor_tensor(part, part, ot[:, h, :], ALU.add)
                    if h == 0:
                        step(ins)
                ins.then_inc(x_ready, 1)
            dve.wait_ge(x_ready, NB)
            dve.wait_ge(norm2_in, 16)
            step(V.scalar_tensor_tensor(out=mods[:, 4, :], in0=mods[:, 4, :], scalar=1.0, in1=norm2,
                                        op0=ALU.add, op1=ALU.mult))
            dve.wait_ge(ms_a, 3)
            V.tensor_scalar(st[:, 4:8], st[:, 0:4], 1.0 / D, EPS, ALU.mult, ALU.add).then_inc(ms_v, 1)
            dve.wait_ge(ms_a, 4)
            step(V.reciprocal(st[:, 12:16], st[:, 8:12]))
            for b in range(NB):
                step(V.scalar_tensor_tensor(out=h2[:, b, :], in0=xt[:, b, :], scalar=st[:, 12 + b:13 + b],
                                            in1=mods[:, 4, :], op0=ALU.mult, op1=ALU.mult))
                V.tensor_tensor(h2[:, b, :], h2[:, b, :], mods[:, 3, :], ALU.add).then_inc(h2_ready, 1)

            best = v3(T1, 2 * PH, PK)
            where_f = v3(T1, 2 * PH, PK, 512)
            where_u = T1[:, 256:512].bitcast(u32).rearrange("p (a b) -> p a b", b=PK)
            top = v3(T1, PH, PK, 768)
            pos = T1[:, 896:1024].bitcast(u32)
            pos3 = pos.rearrange("p (a b) -> p a b", b=PK)
            part_u = T1[:, 1024:1152].bitcast(u32)
            part_f = T1[:, 1152:1280]
            first, second = T1[:, 1536:1664], T1[:, 1664:1792]
            left = T2[:, 0:256]
            hk = PH * PK

            def best16(values, numbers, src, rest):
                step(V.max(values[:, 0:8], src))
                step(V.max_index(numbers[:, 0:8], values[:, 0:8], src))
                step(V.match_replace(rest, values[:, 0:8], src, TAKEN))
                step(V.max(values[:, 8:16], rest))
                step(V.max_index(numbers[:, 8:16], values[:, 8:16], rest))

            def key_of(result, half):
                oh3 = onehot.rearrange("p (q m) -> p q m", m=PK)
                step(V.tensor_copy(part_f, part_u))
                step(V.tensor_tensor(oh3, part_f.unsqueeze(2).broadcast_to([P, hk, PK]),
                                     io16[:, :].unsqueeze(1).broadcast_to([P, hk, PK]), ALU.is_equal))
                oh4 = onehot.rearrange("p (h k m) -> p h k m", h=PH, k=PK)
                keys = where_f.rearrange("p (h s) m -> p h s m", s=2)[:, :, half:half + 1, :]
                step(V.tensor_tensor(oh4, oh4, keys.broadcast_to([P, PH, PK, PK]), ALU.mult))
                step(V.tensor_reduce(result, oh3, AX.X, ALU.add))

            def route(b):
                sc = scores(b)
                for j in range(2 * PH):
                    best16(best[:, j, :], where_u[:, j, :], sc[:, j, :], left[:, 0:NKEYS])
                step(V.tensor_copy(where_f, where_u))
                two = best.rearrange("p (h s) k -> p h s k", s=2)
                step(V.tensor_tensor(cand.rearrange("p (h a c) -> p h a c", h=PH, a=PK),
                                     two[:, :, 0, :].unsqueeze(3).broadcast_to([P, PH, PK, PK]),
                                     two[:, :, 1:2, :].broadcast_to([P, PH, PK, PK]), ALU.add))
                for h in range(PH):
                    best16(top[:, h, :], pos3[:, h, :], cand[:, h * PK * PK:(h + 1) * PK * PK], left)
                step(V.tensor_scalar(part_u, pos, 4, None, ALU.logical_shift_right))
                key_of(first, 0)
                step(V.tensor_scalar(part_u, pos, PK - 1, None, ALU.bitwise_and))
                key_of(second, 1)
                half = slice((b % 2) * P, (b % 2) * P + P)
                g3 = gates[:, half].rearrange("p (h k) -> p h k", k=PK)
                step(V.scalar_tensor_tensor(out=ei[:, half], in0=first, scalar=float(NKEYS), in1=second,
                                            op0=ALU.mult, op1=ALU.add))
                V.tensor_tensor(g3, top, top[:, :, 0:1].broadcast_to([P, PH, PK]), ALU.subtract).then_inc(route_e, 1)
                dve.wait_ge(route_x, b + 1)
                step(V.tensor_reduce(st[:, 240:248], g3, AX.X, ALU.add))
                step(V.reciprocal(st[:, 240:248], st[:, 240:248]))
                V.tensor_tensor(g3, g3, st[:, 240:248].unsqueeze(2).broadcast_to([P, PH, PK]), ALU.mult)\
                 .then_inc(routed, 1)

            def experts(b):
                if b:
                    dve.wait_ge(y_ready, b)
                step(V.memset(acc, 0.0))
                with dve.Fori(0, PH) as i:
                    seen = i * (2 * PK) + (RING + 2 * PK * PH * b)
                    for k in range(PK):
                        dve.wait_ge(row_in[k], i * 32 + (16 + 32 * PH * b))
                        if k >= 2:
                            dve.wait_ge(row_used, seen + (k - 1))
                        V.tensor_tensor_reduce(unread[:, k % 2, :], rows[:, k, :], h2[:, b, :], 1.0, 0.0,
                                               ALU.mult, ALU.add, aw[:, k:k + 1]).then_inc(row_used, 1)
                    dve.wait_ge(gelu_ready, i + (PH * b + 1))
                    V.tensor_tensor(aw[:, 2 * PK:3 * PK], aw[:, PK:2 * PK],
                                    gates[:, bass.ds(i * PK + (b % 2) * P, PK)], ALU.mult).then_inc(weights_set, 1)
                    dve.wait_ge(weights_set, i + (PH * b + 1))
                    for k in range(PK):
                        dve.wait_ge(row_in[k], i * 32 + (32 + 32 * PH * b))
                        if k >= 2:
                            dve.wait_ge(row_used, seen + (PK + k - 1))
                        V.scalar_tensor_tensor(out=acc[:, k % 2, :], in0=rows[:, k, :],
                                               scalar=aw[:, 2 * PK + k:2 * PK + k + 1], in1=acc[:, k % 2, :],
                                               op0=ALU.mult, op1=ALU.add).then_inc(row_used, 1)
                dve.wait_ge(row_used, RING + 2 * PK * PH * (b + 1))
                step(V.tensor_tensor(acc[:, 0, :], acc[:, 0, :], acc[:, 1, :], ALU.add))
                step(V.tensor_tensor(acc[:, 0, :], acc[:, 0, :], mods[:, 5, :], ALU.mult))
                V.tensor_tensor(xt[:, b, :], xt[:, b, :], acc[:, 0, :], ALU.add).then_inc(y_ready, 1)

            fill_read(dve, ("sc", 15))
            V.memset(st[:, 250:251], 0.0).then_inc(row_used, RING)
            route(0)
            for b in range(NB):
                if b + 1 < NB:
                    route(b + 1)
                experts(b)


_INS = ["x", "c", "w_ada", "b_ada", "norm1_g", "norm2_g", "w_in", "hg_lb", "hg_onorm_g", "q_norm_g", "k_norm_g",
        "w_a", "w_b", "w_out", "peer_wq", "peer_subkeys", "peer_u", "peer_v"]


def kernel(**inputs):
    import numpy as _np
    import concourse.bacc as _bacc
    from concourse import mybir as _mybir
    from concourse.bass_utils import run_bass_kernel_spmd as _run

    nc = _bacc.Bacc("TRN2", target_bir_lowering=False, num_devices=1)
    arrays, args = {}, []
    for name in _INS:
        a = _np.ascontiguousarray(inputs[name])
        arrays[f"in_{name}"] = a
        args.append(nc.dram_tensor(f"in_{name}", a.shape, _mybir.dt.from_np(a.dtype), kind="ExternalInput").ap())
    shape = tuple(inputs["x"].shape)
    args.append(nc.dram_tensor("out_0", shape, _mybir.dt.from_np(_np.dtype("float32")), kind="ExternalOutput").ap())
    hybrid_hgrn2_dsa_peer_kernel(nc, *args)
    r = _run(nc, [arrays], core_ids=[0])
    return r.results[0]["out_0"]
```

```python
import concourse.bass as bass
from concourse import mybir
from contextlib import ExitStack


def hybrid_hgrn2_dsa_peer_kernel(
    nc, x, c, w_ada, b_ada, norm1_g, norm2_g, w_in, hg_lb, hg_onorm_g, q_norm_g, k_norm_g,
    w_a, w_b, w_out, peer_wq, peer_subkeys, peer_u, peer_v, out,
):
    fp32 = mybir.dt.float32
    u32 = mybir.dt.uint32
    ALU = mybir.AluOpType
    ACT = mybir.ActivationFunctionType
    AX = mybir.AxisListType

    P = 128
    D = x.shape[2]
    SEQ = x.shape[1]
    NB = SEQ // P
    KD = D // P
    HH, DK, CH = 4, 128, 64
    HGW = HH * DK
    NCH = SEQ // CH
    AH, AG, HD = 8, 2, 64
    AR = AH // AG
    IH = 8
    TOPK = min(256, SEQ // 4)
    PH, PK = 8, 16
    NKEYS = peer_subkeys.shape[3]
    EPS = 1e-6
    IDX_SCALE = (64 ** -0.5) * (IH ** -0.5)
    ATT_SCALE = HD ** -0.5
    TAKEN = -3.0e38
    FUTURE = -1.0e38
    BARRED = -1.0e35
    NW = 2
    RING = 16
    ROUTE_STEPS = 32
    AHEAD = 2
    BANKS = 6
    O_Q, O_F, O_I, O_G = 0, HGW, 2 * HGW, 3 * HGW
    O_AQ = 4 * HGW
    O_IQ = O_AQ + AH * HD + 2 * AG * HD
    O_IK = O_IQ + IH * HD
    O_IW = O_IK + HD
    O_GA = O_IW + IH
    O_GB = O_GA + D

    QUARTERS = [(s0, (s0 // CH + 1) * CH) for s0 in range(0, P, CH // 2)]

    fills, reader = {}, []

    def plan(key, engine):
        fills[key] = len(reader)
        reader.append(engine)

    for n in range(2):
        for h in range(2):
            plan(("ada", n, h), "V")
    for b in range(NB):
        for h in range(2):
            plan(("hT", b, h), "A")
    for j in range(8):
        plan(("qf", j), "A")
    for b in range(NB):
        for h in range(2):
            plan(("att_in", b, h), "A")
    for j in range(5):
        plan(("idx_in", j), "A")
    plan(("iw",), "V")
    for b in range(NB):
        for h in range(2):
            plan(("ig", b, h), "A")
    plan(("kT",), "A")
    for b in range(NB):
        plan(("qT", b), "A")
    for b in range(NB):
        plan(("intra", b), "A")
        plan(("kl", b), "A")
        plan(("dS", 2 * b), "V")
        plan(("dS", 2 * b + 1), "V")
        plan(("o", b), "A")
    for n in range(2, 4):
        for h in range(2):
            plan(("ada", n, h), "V")
    for b in range(NB):
        plan(("yaT", b), "A")
    BESIDE = {(0, 1): [("ada", 4, 0)], (0, 3): [("ada", 4, 1)], (0, 5): [("ada", 5, 0)], (0, 7): [("ada", 5, 1)],
              (1, -1): [("ga", 0, 0), ("ga", 0, 1), ("ga", 1, 0), ("ga", 1, 1)],
              (1, 3): [("ga", 2, 0)], (1, 7): [("ga", 2, 1)],
              (2, -1): [("ga", 3, 0), ("ga", 3, 1), ("gb", 0, 0), ("gb", 0, 1), ("gb", 1, 0)],
              (2, 3): [("gb", 1, 1)], (2, 7): [("gb", 2, 0)],
              (3, -1): [("gb", 2, 1), ("gb", 3, 0), ("gb", 3, 1)]}

    def plan_beside(b, h):
        for key in BESIDE.get((b, h), []):
            plan(key, "V" if key[0] == "ada" else "A")

    for b in range(NB):
        if b:
            for h in range(IH):
                plan(("I", b, h), "A")
            plan_beside(b, -1)
        plan(("S", b, 0), "V")
        for h in range(AH):
            if h + 1 < AH:
                plan(("S", b, h + 1), "V")
            plan(("pT", b, h), "A")
            if h:
                plan(("yb", b, h - 1), "V")
                plan_beside(b, h - 1)
        plan(("yb", b, AH - 1), "V")
        plan_beside(b, AH - 1)
    for b in range(NB):
        plan(("ybT", b), "A")
    for b in range(NB):
        for h in range(2):
            plan(("ya_wa", b, h), "V")
    for b in range(NB + 1):
        for h in range(2):
            if b < NB:
                plan(("yb_wb", b, h), "V")
        for h in range(2):
            if b:
                plan(("mT", b - 1, h), "A")
    for b in range(NB):
        for h in range(2):
            plan(("out", b, h), "V")
    for b in range(NB):
        if b == NB - 1:
            for j in range(4):
                plan(("sk", j), "A")
        for h in range(2):
            plan(("h2T", b, h), "A")
    plan(("qry", 0), "A")
    for j in range(16):
        if j + 1 < 16:
            plan(("qry", j + 1), "A")
        plan(("sc", j), "A")

    def read_by_then(k, engine):
        return sum(e == engine for e in reader[: k + 1])

    ctx = ExitStack()
    with ctx:
        def sb(name, n, dt=fp32, parts=P):
            return ctx.enter_context(nc.sbuf_tensor(name, [parts, n], dt))

        def sem(name):
            return ctx.enter_context(nc.semaphore(name))

        PS = ctx.enter_context(nc.psum_tensor("PS", [P, 8, 512], fp32))

        XR = sb("XR", 4096)
        MODS = sb("MODS", 6144)
        WR = sb("WR", 16384)
        HT = sb("HT", 4096)
        FQ = sb("FQ", 4096)
        VG = sb("VG", 4096)
        AI = sb("AI", 5632)
        T1 = sb("T1", 2048)
        T2 = sb("T2", 2048)
        SM = sb("SM", 2048)
        ident = sb("ident", 128)
        tri = sb("tri", 512)
        dist0 = sb("dist0", 512)
        st = sb("st", 256)
        cs = sb("cs", 32)
        lbt = sb("lbt", 48)
        iw = sb("iw", NB * IH)
        gqk = sb("gqk", 2 * HD)
        selw = sb("selw", 64)
        idx_now = sb("idx_now", 32, u32)
        aw = sb("aw", 64)
        kT = sb("kT", SEQ)
        onorm = sb("onorm", DK)
        io16 = sb("io16", 16)
        g_now = sb("g_now", 16)

        def v3(t, a, b, off=0):
            return t[:, off:off + a * b].rearrange("p (a b) -> p a b", a=a)

        xt = v3(XR, NB, D)
        mods = v3(MODS, 6, D)
        hT = v3(HT, KD, SEQ)
        hq_f, hq_q = v3(FQ, HH, SEQ, 2048), v3(FQ, HH, SEQ)
        vi, gi = v3(VG, NB, HGW), v3(VG, NB, HGW, 2048)
        aq = v3(AI, NB, AH * HD)
        akv = v3(AI, NB, 2 * AG * HD, 2048)
        iqT = v3(AI, 4, SEQ, 3072)
        ikT = AI[:, 5120:5632]
        t1, t2 = v3(T1, HH, SEQ), v3(T2, HH, SEQ)
        t3, t4 = v3(XR, HH, SEQ), v3(XR, HH, SEQ, 2048)
        klT, inT = v3(SM, HH, DK), v3(SM, HH, P, 512)
        state = SM[:, 1024:2048].rearrange("p (v h e) -> p v h e", v=2, h=HH)
        ya = v3(MODS, NB, HGW)
        yb = v3(SM, NB, AH * HD)
        hbuf = v3(VG, 2, D)
        normg = T1[:, 0:D]
        junk = T1[:, D:2 * D]
        squares, k_squares = v3(SM, NB, AH * HD), v3(VG, NB, P)
        qT = v3(AI, NB * AR, P)
        qn = SM[:, 0:NB * AH * HD].rearrange("p (b r g d) -> p b r g d", b=NB, r=AR, g=AG)
        g_sig = v3(FQ, NB, HGW, 2048)
        eps = st[:, 248:249]
        scratch = v3(dist0, HH, DK)
        I_t, wk, dm = VG[:, 0:512], VG[:, 512:1024], VG[:, 1024:1536]
        rl = v3(VG, 2, 512, 1536)
        zz = v3(VG, 2, 512, 2560)
        pp = v3(T2, 2, 512)
        pT = T2[:, 1024:2048].rearrange("p (v s t) -> p v s t", v=2, s=NB)
        m1, m2 = v3(XR, NB, D), v3(FQ, NB, D)
        x2 = v3(VG, NB, D)
        ei, gates = T2[:, 0:512].bitcast(u32), T2[:, 512:1024]
        yaT, ybT = v3(T1, 4, SEQ), v3(T2, 4, SEQ)
        mT = hT
        h2 = v3(XR, NB, D)
        h2T = v3(FQ, KD, SEQ)
        ot = v3(AI, 2, 512, 2048)
        skn, skT = v3(T2, 16, P), v3(SM, 16, P)
        qyT = v3(T1, 2, SEQ)
        norm2 = T1[:, 1024:2048]
        zeros = T2[:, 1024:1536]
        unread = v3(MODS, 2, D)
        diag = v3(SM, PK, P)
        sums = PS[:, BANKS:BANKS + 2, :]

        def scores(b):
            return v3(HT, 16, NKEYS, 2048 * b) if b < 2 else v3(AI, 16, NKEYS, 2048 * (b - 2))

        w_ring = [v3(WR, KD, D, 8192 * s) for s in range(NW)]
        rows = v3(WR, RING, D)

        filled = sem("filled")
        act_read = sem("act_read")
        dve_read = sem("dve_read")
        w_loaded = [sem(f"w_loaded{s}") for s in range(NW)]
        w_first = sem("w_first")
        c_in = sem("c_in")
        small_in = sem("small_in")
        mods_in = sem("mods_in")
        x_in = sem("x_in")
        x_again = sem("x_again")
        norm2_in = sem("norm2_in")
        sk_in = sem("sk_in")
        ikd = sem("ikd")
        const = sem("const")
        v_step = sem("v_step")
        a_step = sem("a_step")
        c_exp = sem("c_exp")
        cs_ready = sem("cs_ready")
        qk_v, qk_a = sem("qk_v"), sem("qk_a")
        x_root = sem("x_root")
        h_ready = sem("h_ready")
        hg_v, hg_a = sem("hg_v"), sem("hg_a")
        f_ready = sem("f_ready")
        masked = sem("masked")
        state_zero = sem("state_zero")
        eps_set = sem("eps_set")
        o_squares, o_sums, o_roots = sem("o_squares"), sem("o_sums"), sem("o_roots")
        ya_ready = sem("ya_ready")
        gate_open = sem("gate_open")
        weights_set = sem("weights_set")
        q_ready = sem("q_ready")
        i_masked = sem("i_masked")
        d_ready, d_masked = sem("d_ready"), sem("d_masked")
        relu_ready, relu_used = sem("relu_ready"), sem("relu_used")
        z_ready, p_ready = sem("z_ready"), sem("p_ready")
        yb_ready = sem("yb_ready")
        m_ready = sem("m_ready")
        x_ready = sem("x_ready")
        h2_ready = sem("h2_ready")
        route_e, route_x = sem("route_e"), sem("route_x")
        route_step = sem("route_step")
        step_seen = sem("step_seen")
        idx_set = sem("idx_set")
        row_in = [sem(f"row_in{s}") for s in range(RING)]
        u_used = sem("u_used")
        v_used = sem("v_used")
        diag_ready = sem("diag_ready")
        summed, sums_read = sem("summed"), sem("sums_read")
        slot_free = sem("slot_free")
        gelu_ready = sem("gelu_ready")
        y_ready = sem("y_ready")
        out_done = sem("out_done")

        block = ctx.enter_context(nc.Block())

        tiles = []
        wt = {}

        def tile(name, src, chunks=KD):
            wt[name] = len(tiles)
            tiles.append((name, src, chunks))

        wav = w_ada[0].rearrange("(k p) n -> p k n", p=P)
        wiv = w_in[0].rearrange("(k p) n -> p k n", p=P)
        for n in range(2):
            tile(f"ada{n}", wav[:, :, n * D:(n + 1) * D])
        tile("qf", wiv[:, :, O_Q:O_I])
        tile("att", wiv[:, :, O_AQ:O_IQ])
        tile("idx", None)
        tile("ig", wiv[:, :, O_I:O_AQ])
        for n in range(2, 6):
            tile(f"ada{n}", wav[:, :, n * D:(n + 1) * D])
        tile("ga", wiv[:, :, O_GA:O_GB])
        tile("gb", wiv[:, :, O_GB:O_GB + D])
        tile("wab", None)
        tile("wout", w_out[0].rearrange("(k p) n -> p k n", p=P))
        wqv = peer_wq[0].rearrange("(k p) n -> p k n", p=P)
        tile("wq0", wqv[:, :, 0:D])
        tile("wq1", wqv[:, :, D:2 * D])
        parts_of = {"idx": 4, "wab": 2}
        last_fill = {"qf": ("qf", 7), "ig": ("ig", NB - 1, 1), "att": ("att_in", NB - 1, 1), "idx": ("iw",),
                     "ga": ("ga", NB - 1, 1), "gb": ("gb", NB - 1, 1), "wab": ("yb_wb", NB - 1, 1),
                     "wout": ("out", NB - 1, 1), "wq0": ("qry", 7), "wq1": ("qry", 15)}
        for n in range(6):
            last_fill[f"ada{n}"] = ("ada", n, 1)

        def tile_loaded(eng, name):
            i = wt[name]
            n = sum(16 * parts_of.get(tiles[j][0], 1) for j in range(i % NW, i + 1, NW))
            eng.wait_ge(w_loaded[i % NW], n)
            return w_ring[i % NW]

        def fill_read(eng, key):
            k = fills[key]
            who = reader[k]
            eng.wait_ge(act_read if who == "A" else dve_read, read_by_then(k, who))

        @block.sync
        def _(sp):
            with nc.allow_non_contiguous_dma(reason="small columns"):
                sp.dma_start(cs[:, 0:KD], c[0].rearrange("(k p) -> p k", p=P)).then_inc(c_in, 16)
                sp.dma_start(lbt[:, 0:8].rearrange("p (l h) -> p l h", l=2),
                             hg_lb.rearrange("l (h p) -> p l h", p=P)).then_inc(c_in, 16)
            sp.dma_start(w_ring[0][:, :, 0:512], tiles[0][1][:, :, 0:512]).then_inc(w_first, 16)
            sp.dma_start(MODS[:, 0:2 * D], b_ada[0:1, 0:2 * D].to_broadcast([P, 2 * D])).then_inc(small_in, 16)
            sp.dma_start(w_ring[0][:, :, 512:D], tiles[0][1][:, :, 512:D]).then_inc(w_loaded[0], 16)
            sp.dma_start(w_ring[1], tiles[1][1]).then_inc(w_loaded[1], 16)
            sp.dma_start(xt, x[0].rearrange("(b p) d -> p b d", p=P)).then_inc(x_in, 16)
            sp.dma_start(normg, norm1_g[0:1, :].to_broadcast([P, D])).then_inc(small_in, 16)
            sp.dma_start(gqk[:, 0:HD], q_norm_g[0:1, :].to_broadcast([P, HD])).then_inc(small_in, 16)
            sp.dma_start(gqk[:, HD:2 * HD], k_norm_g[0:1, :].to_broadcast([P, HD])).then_inc(small_in, 16)
            sp.dma_start(onorm[:, :], hg_onorm_g[0:1, :].to_broadcast([P, DK])).then_inc(small_in, 16)
            for i, (name, src, chunks) in enumerate(tiles):
                if i < NW:
                    continue
                sp.wait_ge(filled, fills[last_fill[tiles[i - NW][0]]] + 1)
                slot, s = w_ring[i % NW], w_loaded[i % NW]
                if name == "idx":
                    n = IH * HD
                    sp.dma_start(slot[:, :, 0:n], wiv[:, :, O_IQ:O_IK]).then_inc(s, 16)
                    sp.dma_start(slot[:, :, n:n + HD], wiv[:, :, O_IK:O_IW]).then_inc(s, 16)
                    sp.dma_start(slot[:, :, n + HD:n + 2 * HD], wiv[:, :, O_IK:O_IW]).then_inc(s, 16)
                    sp.dma_start(slot[:, :, n + 2 * HD:n + 2 * HD + IH], wiv[:, :, O_IW:O_GA]).then_inc(s, 16)
                elif name == "wab":
                    sp.dma_start(slot[:, 0:4, :], w_a[0].rearrange("(k p) n -> p k n", p=P)).then_inc(s, 16)
                    sp.dma_start(slot[:, 4:8, :], w_b[0].rearrange("(k p) n -> p k n", p=P)).then_inc(s, 16)
                else:
                    sp.dma_start(slot[:, :, 0:src.shape[2]], src).then_inc(s, 16)
                if name == "att":
                    sp.dma_start(MODS[:, 2 * D:6 * D],
                                 b_ada[0:1, 2 * D:6 * D].to_broadcast([P, 4 * D])).then_inc(mods_in, 16)
                if name == "wout":
                    sp.wait_ge(yb_ready, 1)
                    sp.dma_start(x2, x[0].rearrange("(b p) d -> p b d", p=P)).then_inc(x_again, 16)
                    sp.wait_ge(filled, fills[("yb_wb", NB - 1, 1)] + 1)
                    sp.dma_start(norm2, norm2_g[0:1, :].to_broadcast([P, D])).then_inc(norm2_in, 16)
                    sp.dma_start(skn, peer_subkeys[0].rearrange("h s n d -> n (h s) d")).then_inc(sk_in, 16)
            for b in range(NB):
                sp.wait_ge(y_ready, b + 1)
                sp.dma_start(out[0, b * P:(b + 1) * P, :], x2[:, b, :]).then_inc(out_done, 16)
            sp.wait_ge(out_done, 16 * NB)

        @block.gpsimd
        def _(pool):
            pool.memset(ident[:, :], 0.0).then_inc(const, 1)
            pool.wait_ge(const, 1)
            pool.affine_select(out=ident[:, :], in_=ident[:, :], compare_op=ALU.not_equal, fill=1.0,
                               base=0, pattern=[[-1, P]], channel_multiplier=1).then_inc(const, 1)
            pool.memset(tri[:, :], 1.0).then_inc(const, 1)
            pool.wait_ge(const, 3)
            pool.memset(tri[:, 0:SEQ:CH], 0.0).then_inc(const, 1)
            pool.wait_ge(filled, fills[("qT", NB - 1)] + 1)
            pool.memset(inT, 0.0).then_inc(const, 1)
            pool.iota(io16[:, :], pattern=[[1, PK]], base=0, channel_multiplier=0,
                      allow_small_or_imprecise_dtypes=True).then_inc(const, 1)
            for b in range(NB):
                fill_read(pool, ("intra", b))
                pool.affine_select(out=inT, in_=inT, compare_op=ALU.is_ge, fill=0.0, base=0,
                                   pattern=[[0, HH], [1, P]], channel_multiplier=-1).then_inc(masked, 1)
            fill_read(pool, ("dS", NCH - 1))
            pool.iota(dist0[:, :], pattern=[[1, SEQ]], base=0, channel_multiplier=-1,
                      allow_small_or_imprecise_dtypes=True).then_inc(const, 1)
            for b in range(NB):
                if b:
                    pool.wait_ge(relu_used, IH * b)
                    last = I_t[:, b * P:(b + 1) * P]
                    pool.affine_select(out=last, in_=last, compare_op=ALU.is_ge, fill=FUTURE, base=0,
                                       pattern=[[-1, P]], channel_multiplier=1).then_inc(i_masked, 1)
                else:
                    pool.wait_ge(d_ready, 1)
                    pool.affine_select(out=dm[:, 0:P], in_=dm[:, 0:P], compare_op=ALU.is_ge, fill=BARRED,
                                       base=0, pattern=[[-1, P]], channel_multiplier=1).then_inc(d_masked, 1)
            pool.wait_ge(filled, fills[("sk", 3)] + 1)
            pool.memset(zeros, 0.0).then_inc(const, 1)

            def take_numbers(head, parity):
                now = idx_now[:, parity * PK:(parity + 1) * PK]
                pool.wait_ge(route_step, head * ROUTE_STEPS + ROUTE_STEPS)
                pool.sem_inc(slot_free, 1)
                pool.tensor_copy(now, ei[:, bass.ds(head * PK, PK)]).then_inc(idx_set, 1)
                pool.wait_ge(idx_set, head + 1)
                return now

            def gather(src, k, now):
                pool.sem_inc(slot_free, 1)
                pool.indirect_dma_start(
                    rows[:, k, :], None, src[0],
                    bass.IndirectOffsetOnAxis(ap=now[:, k:k + 1], axis=0)).then_inc(row_in[k], 16)

            def gather_head(head, parity):
                now = take_numbers(head, parity)
                for src, used, n in ((peer_u, v_used, 1 - PK), (peer_v, u_used, 1)):
                    for k in range(PK):
                        pool.wait_ge(used, PK * head + k + n)
                        gather(src, k, now)

            now = take_numbers(0, 0)
            pool.wait_ge(filled, fills[("qry", 7)] + 1)
            for half in range(2):
                if half:
                    pool.wait_ge(filled, fills[("qry", 15)] + 1)
                ks = range(half * PK // 2, (half + 1) * PK // 2)
                for k in ks:
                    gather(peer_u, k, now)
                for k in ks:
                    pool.wait_ge(u_used, k + 1)
                    gather(peer_v, k, now)
            gather_head(1, 1)
            with pool.Fori(1, NB * PH // 2) as i:
                for u in range(2):
                    gather_head(2 * i + u, u)

        @block.scalar
        def _(act):
            chain = [0]

            def step(ins):
                chain[0] += 1
                ins.then_inc(a_step, 1)
                act.wait_ge(a_step, chain[0])

            def take(key, out_ap, in_ap):
                k = fills[key]
                act.wait_ge(filled, k + 1)
                nc.scalar.activation(out_ap, in_ap(PS[:, k % BANKS, :]), ACT.Copy).then_inc(act_read, 1)

            whole = lambda ps: ps
            quads = lambda ps: ps.rearrange("p (a b) -> p a b", a=4)
            act.wait_ge(c_in, 32)
            nc.scalar.activation(cs[:, KD:2 * KD], cs[:, 0:KD], ACT.Sigmoid).then_inc(c_exp, 1)
            act.wait_ge(cs_ready, 1)
            nc.scalar.activation(lbt[:, 8:16], lbt[:, 16:24], ACT.Exp).then_inc(c_exp, 1)
            act.wait_ge(x_in, 16)
            for b in range(NB):
                step(nc.scalar.activation(junk, xt[:, b, :], ACT.Square, accum_out=st[:, b:b + 1]))
            act.wait_ge(eps_set, 1)
            nc.scalar.activation(st[:, 8:12], st[:, 0:4], ACT.Sqrt, bias=eps, scale=1.0 / D).then_inc(x_root, 1)
            for b in range(NB):
                for h in range(2):
                    take(("hT", b, h), hT[:, 4 * h:4 * h + 4, b * P:(b + 1) * P], quads)
            for j in range(8):
                take(("qf", j), hq_q[:, j, :] if j < 4 else hq_f[:, j - 4, :], whole)
            fill_read(act, ("qf", 7))
            nc.scalar.activation(hq_f, hq_f, ACT.Sigmoid).then_inc(hg_a, 1)
            act.wait_ge(hg_v, 1)
            nc.scalar.activation(t2, hq_q, ACT.Sigmoid).then_inc(hg_a, 1)
            act.wait_ge(f_ready, HH)
            nc.scalar.activation(t1, hq_f, ACT.Ln).then_inc(hg_a, 1)

            def take_att(b):
                take(("att_in", b, 0), aq[:, b, :], whole)
                take(("att_in", b, 1), akv[:, b, :], lambda ps: ps[:, 0:256])

            take_att(0)
            take_att(1)
            act.wait_ge(hg_v, 3)
            step(nc.scalar.activation(t3, t1, ACT.Exp))
            step(nc.scalar.activation(t4, t2, ACT.Exp))
            nc.scalar.activation(t1, t1, ACT.Exp, scale=-1.0).then_inc(hg_a, 1)
            act.wait_ge(hg_v, 4)
            step(nc.scalar.activation(lbt[:, 16:48], st[:, 128:160], ACT.Exp))
            nc.scalar.activation(t2, t2, ACT.Exp).then_inc(hg_a, 1)
            take_att(2)
            take_att(3)
            fill_read(act, ("att_in", NB - 1, 1))
            step(nc.scalar.activation(squares, aq, ACT.Square))
            nc.scalar.activation(k_squares, akv[:, :, 0:P], ACT.Square).then_inc(qk_a, 1)
            for j in range(5):
                take(("idx_in", j), iqT[:, j, :] if j < 4 else ikT, whole)
            act.wait_ge(qk_v, 1)
            nc.scalar.activation(st[:, 184:224], st[:, 184:224], ACT.Sqrt).then_inc(qk_a, 1)
            for b in range(NB):
                for h in range(2):
                    take(("ig", b, h), (vi, gi)[h][:, b, :], whole)
                fill_read(act, ("ig", b, 1))
                if b == 0:
                    act.wait_ge(hg_v, 7)
                nc.scalar.activation(g_sig[:, b, :], gi[:, b, :], ACT.Sigmoid).then_inc(hg_a, 1)
            take(("kT",), kT[:, :], whole)
            for b in range(NB):
                take(("qT", b), qT[:, 4 * b:4 * b + 4, :], quads)

            def root(b):
                act.wait_ge(o_sums, b + 1)
                nc.scalar.activation(st[:, 64 + HH * b:64 + HH * (b + 1)], st[:, 64 + HH * b:64 + HH * (b + 1)],
                                     ACT.Sqrt, bias=eps, scale=1.0 / DK).then_inc(o_roots, 1)

            for b in range(NB):
                if b:
                    act.wait_ge(filled, fills[("o", b - 1)] + 1)
                k = fills[("intra", b)]
                act.wait_ge(filled, k + 1)
                if b == 0:
                    act.wait_ge(const, 6)
                for s0, c1 in QUARTERS:
                    ins = nc.scalar.activation(inT[s0:s0 + CH // 2, :, s0:c1],
                                               quads(PS[s0:s0 + CH // 2, k % BANKS, :])[:, :, s0:c1], ACT.Copy)
                ins.then_inc(act_read, 1)
                take(("kl", b), klT, quads)
                if b:
                    root(b - 1)
                take(("o", b), ya[:, b, :], whole)
                if b == 0:
                    act.wait_ge(hg_v, 7 + NB)
                fill_read(act, ("o", b))
                nc.scalar.activation(g_sig[:, b, :], ya[:, b, :], ACT.Square).then_inc(o_squares, 1)
            root(NB - 1)
            act.wait_ge(ya_ready, 1)
            for b in range(NB):
                take(("yaT", b), yaT[:, :, b * P:(b + 1) * P], quads)

            def beside(b, h):
                for key in BESIDE.get((b, h), []):
                    if key[0] != "ada":
                        m = (m1 if key[0] == "ga" else m2)[:, key[1], 512 * key[2]:512 * key[2] + 512]
                        take(key, m, whole)

            nI = 0
            n = 0

            def exp_row(b, h, n):
                W = (b + 1) * P
                act.wait_ge(z_ready, n + 1)
                if n >= 2:
                    act.wait_ge(filled, fills[("pT", (n - 2) // AH, (n - 2) % AH)] + 1)
                nc.scalar.activation(pp[:, n % 2, 0:W], zz[:, n % 2, 0:W], ACT.Exp,
                                     bias=st[:, 16 + n:17 + n], accum_out=st[:, 64 + n:65 + n]).then_inc(p_ready, 1)

            for b in range(NB):
                W = (b + 1) * P
                if b:
                    for h in range(IH):
                        k = fills[("I", b, h)]
                        act.wait_ge(filled, k + 1)
                        if nI >= 2:
                            act.wait_ge(relu_used, nI - 1)
                        nc.scalar.activation(rl[:, nI % 2, 0:W], PS[:, k % BANKS, 0:W], ACT.Relu).then_inc(act_read, 1)
                        nI += 1
                beside(b, -1)
                exp_row(b, 0, n)
                for h in range(AH):
                    if h + 1 < AH:
                        exp_row(b, h + 1, n + 1)
                    if n >= 2:
                        act.wait_ge(filled, fills[("yb", (n - 2) // AH, (n - 2) % AH)] + 1)
                    take(("pT", b, h), pT[:, n % 2, 0:b + 1, :],
                         lambda ps: ps[:, 0:W].rearrange("p (a b) -> p a b", a=W // P))
                    n += 1
                    if h:
                        beside(b, h - 1)
                beside(b, AH - 1)
            for b in range(NB):
                if b == 0:
                    act.wait_ge(filled, fills[("yb", NB - 1, AH - 1)] + 1)
                take(("ybT", b), ybT[:, :, b * P:(b + 1) * P], quads)
            fill_read(act, ("gb", NB - 1, 1))
            for m in (m1, m2):
                for b in range(NB):
                    nc.scalar.activation(m[:, b, :], m[:, b, :], ACT.Sigmoid).then_inc(gate_open, 1)
            for b in range(NB):
                for h in range(2):
                    if b == 0 and h == 0:
                        act.wait_ge(filled, fills[("gb", NB - 1, 1)] + 1)
                    take(("mT", b, h), mT[:, 4 * h:4 * h + 4, b * P:(b + 1) * P], quads)
            for b in range(NB):
                act.wait_ge(x_ready, b + 1)
                step(nc.scalar.activation(T1[:, 0:D], x2[:, b, :], ACT.Square, accum_out=st[:, b:b + 1]))
                nc.scalar.activation(st[:, 8 + b:9 + b], st[:, b:b + 1], ACT.Sqrt, bias=eps,
                                     scale=1.0 / D).then_inc(x_root, 1)
            for b in range(NB):
                if b == NB - 1:
                    for j in range(4):
                        take(("sk", j), skT[:, 4 * j:4 * j + 4, :], quads)
                for h in range(2):
                    take(("h2T", b, h), h2T[:, 4 * h:4 * h + 4, b * P:(b + 1) * P], quads)

            def take_q(j):
                if j == 0:
                    act.wait_ge(h2_ready, NB)
                if j >= 2:
                    act.wait_ge(filled, fills[("sc", j - 2)] + 1)
                take(("qry", j), qyT[:, j % 2, :], whole)

            def gates_exp(n):
                act.wait_ge(route_e, n)
                nc.scalar.activation(g_now[:, :], g_now[:, :], ACT.Exp).then_inc(route_x, 1)

            take_q(0)
            for j in range(16):
                if j + 1 < 16:
                    take_q(j + 1)
                if j in (4, 6):
                    gates_exp(j // 2 - 1)
                k = fills[("sc", j)]
                act.wait_ge(filled, k + 1)
                ps = quads(PS[:, k % BANKS, :])
                nc.scalar.activation(HT[:, :].rearrange("p (b j n) -> p b j n", b=2, j=16)[:, :, j, :],
                                     ps[:, 0:2, :], ACT.Copy)
                nc.scalar.activation(AI[:, 0:4096].rearrange("p (b j n) -> p b j n", b=2, j=16)[:, :, j, :],
                                     ps[:, 2:4, :], ACT.Copy).then_inc(act_read, 1)
            def weigh(i, more):
                act.wait_ge(u_used, i * PK + PK)
                nc.scalar.activation(aw[:, PK:2 * PK], aw[:, 0:PK], ACT.Gelu).then_inc(gelu_ready, 1)
                act.wait_ge(weights_set, i + 1)
                for k in range(PK):
                    nc.scalar.activation(diag[:, k, :], ident[:, :], ACT.Copy,
                                         scale=aw[:, 2 * PK + k:2 * PK + k + 1]).then_inc(diag_ready, 1)
                if more:
                    gates_exp(i + (1 + AHEAD))

            with act.Fori(0, NB * PH - AHEAD) as i:
                weigh(i, True)
            with act.Fori(NB * PH - AHEAD, NB * PH) as i:
                weigh(i, False)

        @block.tensor
        def _(pe):
            def bank(key):
                k = fills[key]
                if k >= BANKS:
                    who = reader[k - BANKS]
                    pe.wait_ge(act_read if who == "A" else dve_read, read_by_then(k - BANKS, who))
                return PS[:, k % BANKS, :]

            def done(ins):
                ins.then_inc(filled, 1)

            def product(key, parts, n=512, ps=None):
                ps = bank(key) if ps is None else ps
                for i, (lhsT, rhs) in enumerate(parts):
                    ins = nc.tensor.matmul(ps[:, 0:n], lhsT, rhs, start=i == 0, stop=i == len(parts) - 1)
                return ins

            def turned(key, ins_):
                ps = bank(key)
                for i, a in enumerate(ins_):
                    last = nc.tensor.transpose(ps[:, i * P:(i + 1) * P], a, ident[:, :])
                done(last)

            pe.wait_ge(const, 2)
            pe.wait_ge(cs_ready, 2)

            def c_column(k):
                return cs[:, KD + k:KD + k + 1].broadcast_to([P, P])

            def ada(n):
                if n:
                    w = tile_loaded(pe, f"ada{n}")
                for h in range(2):
                    if n == 0 and h == 0:
                        pe.wait_ge(w_first, 16)
                        w = w_ring[0]
                    elif n == 0:
                        tile_loaded(pe, "ada0")
                    done(product(("ada", n, h), [(c_column(k), w[:, k, 512 * h:512 * h + 512]) for k in range(KD)]))

            def token_major(key, w, src, halves, chunks=KD, k0=0, blocks=range(NB)):
                for b in blocks:
                    for h, n in enumerate(halves):
                        done(product((key, b, h), [(src[:, k, b * P:(b + 1) * P], w[:, k0 + k, 512 * h:512 * h + n])
                                                   for k in range(chunks)], n))

            ada(0)
            ada(1)
            for b in range(NB):
                pe.wait_ge(h_ready, b + 1)
                for h in range(2):
                    turned(("hT", b, h), [hbuf[:, b % 2, (4 * h + i) * P:(4 * h + i + 1) * P] for i in range(4)])
            w = tile_loaded(pe, "qf")
            fill_read(pe, ("hT", NB - 1, 1))
            for j in range(8):
                done(product(("qf", j), [(w[:, k, j * P:(j + 1) * P], hT[:, k, :]) for k in range(KD)]))
            token_major("att_in", tile_loaded(pe, "att"), hT, (512, 256))
            w = tile_loaded(pe, "idx")
            for j in range(5):
                done(product(("idx_in", j), [(w[:, k, j * P:(j + 1) * P], hT[:, k, :]) for k in range(KD)]))
            ps = bank(("iw",))
            for b in range(NB):
                last = product(None, [(hT[:, k, b * P:(b + 1) * P], w[:, k, 5 * P:5 * P + IH]) for k in range(KD)],
                               IH, ps[:, b * IH:(b + 1) * IH])
            done(last)
            token_major("ig", tile_loaded(pe, "ig"), hT, (512, 512))
            pe.wait_ge(q_ready, 1)
            turned(("kT",), [akv[:, b, 0:P] for b in range(NB)])
            for b in range(NB):
                turned(("qT", b), [qn[:, b, r, :, :].rearrange("p g d -> p (g d)") for r in range(AR)])
            pe.wait_ge(hg_v, 7)
            fill_read(pe, ("ig", NB - 1, 1))
            for b in range(NB):
                t = slice(b * P, (b + 1) * P)
                ps = bank(("intra", b))
                for h in range(HH):
                    for s0, c1 in QUARTERS:
                        last = nc.tensor.matmul(ps[s0:s0 + CH // 2, h * P + s0:h * P + c1],
                                                t1[:, h, b * P + s0:b * P + s0 + CH // 2],
                                                t3[:, h, b * P + s0:b * P + c1], start=True, stop=True)
                done(last)
                turned(("kl", b), [t2[:, h, t] for h in range(HH)])
                fill_read(pe, ("kl", b))
                for j in range(2):
                    ps = bank(("dS", 2 * b + j))
                    s = slice(j * CH, (j + 1) * CH)
                    for h in range(HH):
                        e = slice(h * DK, (h + 1) * DK)
                        last = nc.tensor.matmul(ps[:, e], klT[s, h, :], vi[s, b, e], start=True, stop=True)
                    done(last)
                pe.wait_ge(masked, b + 1)
                pe.wait_ge(state_zero, 1)
                fill_read(pe, ("dS", 2 * b))
                ps = bank(("o", b))
                for h in range(HH):
                    e = slice(h * DK, (h + 1) * DK)
                    nc.tensor.matmul(ps[:, e], inT[:, h, :], vi[:, b, e], start=True, stop=False)
                    nc.tensor.matmul(ps[:, e], hq_q[:, h, t], state[:, 0, h, :], start=False, stop=False)
                    last = nc.tensor.matmul(ps[:, e], t4[:, h, t], state[:, 1, h, :], start=False, stop=True)
                done(last)
            ada(2)
            ada(3)
            pe.wait_ge(ya_ready, 1)
            for b in range(NB):
                turned(("yaT", b), [ya[:, b, i * P:(i + 1) * P] for i in range(4)])

            def beside(b, h):
                for key in BESIDE.get((b, h), []):
                    w = tile_loaded(pe, f"ada{key[1]}" if key[0] == "ada" else key[0])
                    cols = slice(512 * key[2], 512 * key[2] + 512)
                    lhsT = [c_column(k) if key[0] == "ada" else hT[:, k, key[1] * P:(key[1] + 1) * P]
                            for k in range(KD)]
                    done(product(key, [(lhsT[k], w[:, k, cols]) for k in range(KD)]))

            def att_scores(b, h):
                g, r = h // AR, h % AR
                q = qT[g * HD:(g + 1) * HD, b * AR + r, :]
                done(product(("S", b, h), [(q, kT[g * HD:(g + 1) * HD, 0:(b + 1) * P])], (b + 1) * P))

            def att_out(b, h):
                g, n = h // AR, AH * b + h
                fill_read(pe, ("pT", b, h))
                done(product(("yb", b, h), [(pT[:, n % 2, i, :], akv[:, i, P + g * HD:P + (g + 1) * HD])
                                            for i in range(b + 1)], HD))

            n = 0
            for b in range(NB):
                if b:
                    for h in range(IH):
                        s = slice((h % 2) * HD, (h % 2 + 1) * HD)
                        done(product(("I", b, h), [(iqT[s, h // 2, b * P:(b + 1) * P], ikT[s, 0:(b + 1) * P])],
                                     (b + 1) * P))
                    beside(b, -1)
                att_scores(b, 0)
                for h in range(AH):
                    if h + 1 < AH:
                        att_scores(b, h + 1)
                    pe.wait_ge(p_ready, n + 1)
                    turned(("pT", b, h), [pp[:, n % 2, i * P:(i + 1) * P] for i in range(b + 1)])
                    if h:
                        att_out(b, h - 1)
                        beside(b, h - 1)
                    n += 1
                att_out(b, AH - 1)
                beside(b, AH - 1)
            pe.wait_ge(yb_ready, 1)
            for b in range(NB):
                turned(("ybT", b), [yb[:, b, i * P:(i + 1) * P] for i in range(4)])
            w = tile_loaded(pe, "wab")
            fill_read(pe, ("ybT", NB - 1))
            token_major("ya_wa", w, yaT, (512, 512), 4, 0)

            def merged_turned(b):
                for h in range(2):
                    pe.wait_ge(m_ready, 2 * b + h + 1)
                    turned(("mT", b, h), [m1[:, b, (4 * h + i) * P:(4 * h + i + 1) * P] for i in range(4)])

            for b in range(NB):
                token_major("yb_wb", w, ybT, (512, 512), 4, 4, [b])
                if b:
                    merged_turned(b - 1)
            merged_turned(NB - 1)
            w = tile_loaded(pe, "wout")
            for b in range(NB):
                fill_read(pe, ("mT", b, 1))
                token_major("out", w, mT, (512, 512), blocks=[b])
            for b in range(NB):
                if b == NB - 1:
                    pe.wait_ge(sk_in, 16)
                    for j in range(4):
                        turned(("sk", j), [skn[:, 4 * j + i, :] for i in range(4)])
                pe.wait_ge(h2_ready, b + 1)
                for h in range(2):
                    turned(("h2T", b, h), [h2[:, b, (4 * h + i) * P:(4 * h + i + 1) * P] for i in range(4)])
            fill_read(pe, ("h2T", NB - 1, 1))

            def query(j):
                w = tile_loaded(pe, f"wq{j // 8}")
                done(product(("qry", j), [(w[:, k, (j % 8) * P:(j % 8 + 1) * P], h2T[:, k, :]) for k in range(KD)]))

            query(0)
            for j in range(16):
                if j + 1 < 16:
                    query(j + 1)
                fill_read(pe, ("qry", j))
                ps = bank(("sc", j))
                for b in range(NB):
                    last = nc.tensor.matmul(ps[:, b * P:(b + 1) * P], qyT[:, j % 2, b * P:(b + 1) * P], skT[:, j, :],
                                            start=True, stop=True)
                done(last)

            pe.wait_ge(const, 8)
            for b in range(NB):
                if b:
                    pe.wait_ge(sums_read, b)
                for h in range(2):
                    nc.tensor.matmul(sums[:, h, :], zeros[:, 0:P], zeros[:, :], start=True, stop=False)
                with pe.Fori(PH * b, PH * (b + 1)) as i:
                    for k in range(PK):
                        pe.wait_ge(row_in[k], i * 32 + 32)
                        pe.wait_ge(diag_ready, i * PK + (k + 1))
                        for h in range(2):
                            last = nc.tensor.matmul(sums[:, h, :], diag[:, k, :], rows[:, k, 512 * h:512 * h + 512],
                                                    start=False, stop=False)
                        last.then_inc(v_used, 1)
                for h in range(2):
                    last = nc.tensor.matmul(sums[:, h, :], zeros[:, 0:P], zeros[:, :], start=False, stop=True)
                last.then_inc(summed, 1)

        @block.vector
        def _(dve):
            V = nc.vector
            chain = [0]

            def step(ins):
                chain[0] += 1
                ins.then_inc(v_step, 1)
                dve.wait_ge(v_step, chain[0])

            def ready(key):
                k = fills[key]
                dve.wait_ge(filled, k + 1)
                return PS[:, k % BANKS, :]

            def take(ins):
                ins.then_inc(dve_read, 1)

            def one_over_one_plus(t):
                step(V.tensor_scalar(t, t, 1.0, None, ALU.add))
                step(V.reciprocal(t, t))

            def spread(t, shape):
                return t.broadcast_to(shape)

            V.memset(eps, EPS).then_inc(eps_set, 1)
            dve.wait_ge(c_in, 32)
            step(V.tensor_tensor(lbt[:, 40:44], lbt[:, 0:4], lbt[:, 4:8], ALU.max))
            V.tensor_tensor(lbt[:, 16:24].rearrange("p (l h) -> p l h", l=2),
                            lbt[:, 0:8].rearrange("p (l h) -> p l h", l=2),
                            lbt[:, 40:44].unsqueeze(1).broadcast_to([P, 2, 4]), ALU.subtract).then_inc(cs_ready, 1)
            dve.wait_ge(c_exp, 1)
            V.tensor_tensor(cs[:, KD:2 * KD], cs[:, KD:2 * KD], cs[:, 0:KD], ALU.mult).then_inc(cs_ready, 1)
            dve.wait_ge(c_exp, 2)
            step(V.tensor_tensor(lbt[:, 16:20], lbt[:, 8:12], lbt[:, 12:16], ALU.add))
            step(V.reciprocal(lbt[:, 16:20], lbt[:, 16:20]))
            step(V.tensor_tensor(lbt[:, 0:4], lbt[:, 8:12], lbt[:, 16:20], ALU.mult))
            step(V.tensor_scalar(lbt[:, 4:8], lbt[:, 0:4], -1.0, 1.0, ALU.mult, ALU.add))
            def ada_half(n, h):
                part = mods[:, n, 512 * h:512 * h + 512]
                take(V.tensor_tensor(part, part, ready(("ada", n, h)), ALU.add))

            def ada(n):
                ada_half(n, 0)
                ada_half(n, 1)

            dve.wait_ge(small_in, 80)
            ada(0)
            ada(1)
            fill_read(dve, ("ada", 1, 1))
            dve.wait_ge(x_root, 1)
            step(V.reciprocal(st[:, 12:16], st[:, 8:12]))
            step(V.scalar_tensor_tensor(out=mods[:, 1, :], in0=mods[:, 1, :], scalar=1.0, in1=normg,
                                        op0=ALU.add, op1=ALU.mult))
            for b in range(NB):
                if b >= 2:
                    dve.wait_ge(filled, fills[("hT", b - 2, 1)] + 1)
                step(V.scalar_tensor_tensor(out=hbuf[:, b % 2, :], in0=xt[:, b, :], scalar=st[:, 12 + b:13 + b],
                                            in1=mods[:, 1, :], op0=ALU.mult, op1=ALU.mult))
                V.tensor_tensor(hbuf[:, b % 2, :], hbuf[:, b % 2, :], mods[:, 0, :], ALU.add).then_inc(h_ready, 1)
            dve.wait_ge(filled, fills[("ada", 1, 1)] + 1)
            dve.wait_ge(h_ready, NB)
            V.memset(st[:, 250:251], 0.0).then_inc(hg_v, 1)
            dve.wait_ge(hg_a, 1)
            for h in range(HH):
                V.tensor_scalar(hq_f[:, h, :], hq_f[:, h, :], lbt[:, 4 + h:5 + h], lbt[:, h:h + 1],
                                ALU.mult, ALU.add).then_inc(f_ready, 1)
            dve.wait_ge(hg_a, 2)
            V.tensor_tensor(hq_q, hq_q, t2, ALU.mult).then_inc(hg_v, 1)
            dve.wait_ge(hg_v, 2)
            dve.wait_ge(hg_a, 3)
            step(V.tensor_scalar(hq_f, hq_f, -1.0, 1.0, ALU.mult, ALU.add))
            dve.wait_ge(const, 4)
            for h in range(HH):
                step(V.tensor_tensor_scan(t2[:, h, :], tri[:, :], t1[:, h, :], 0.0, ALU.mult, ALU.add))
            chunks = lambda t: t.rearrange("p h (n c) -> p (h n) c", c=CH)
            bl = st[:, 128:160]
            bm = st[:, 96:128]
            step(V.tensor_copy(bl.unsqueeze(2), chunks(t2)[:, :, CH - 1:CH]))
            step(V.tensor_copy(bm.unsqueeze(2), chunks(t2)[:, :, CH // 2 - 1:CH // 2]))
            V.tensor_tensor(chunks(t1), chunks(t2), bm.unsqueeze(2).broadcast_to([P, HH * NCH, CH]),
                            ALU.subtract).then_inc(hg_v, 1)
            dve.wait_ge(hg_a, 4)
            V.tensor_tensor(chunks(t2), bl.unsqueeze(2).broadcast_to([P, HH * NCH, CH]), chunks(t2),
                            ALU.subtract).then_inc(hg_v, 1)
            V.tensor_tensor(t1, hq_f, t1, ALU.mult).then_inc(hg_v, 1)
            step(V.tensor_tensor(t3, hq_q, t3, ALU.mult))
            step(V.tensor_tensor(t4, hq_q, t4, ALU.mult))
            even = lambda t: t.rearrange("p h (n j c) -> p (h n) j c", j=2, c=CH)[:, :, 0, :]
            odd = lambda t: t.rearrange("p h (n j c) -> p (h n) j c", j=2, c=CH)[:, :, 1, :]
            step(V.tensor_copy(even(hq_q), even(t4)))
            step(V.memset(odd(hq_q), 0.0))
            V.memset(even(t4), 0.0).then_inc(hg_v, 1)
            dve.wait_ge(hg_a, 5)
            V.tensor_tensor(t2, hq_f, t2, ALU.mult).then_inc(hg_v, 1)
            q4 = aq.rearrange("p b (h e) -> p (b h) e", h=AH)
            k4 = akv[:, :, 0:P].rearrange("p b (g d) -> p b g d", g=AG)
            k_rms = st[:, 216:224].rearrange("p (b g) -> p b g", b=NB)
            dve.wait_ge(qk_a, 1)
            step(V.tensor_reduce(st[:, 184:216], squares.rearrange("p b (h e) -> p (b h) e", h=AH), AX.X, ALU.add))
            step(V.tensor_reduce(k_rms, k_squares.rearrange("p b (g e) -> p b g e", g=AG), AX.X, ALU.add))
            V.tensor_scalar(st[:, 184:224], st[:, 184:224], 1.0 / HD, EPS, ALU.mult, ALU.add).then_inc(qk_v, 1)
            step(V.tensor_scalar(gqk[:, 0:HD], gqk[:, 0:HD], ATT_SCALE, None, ALU.mult))
            dve.wait_ge(qk_a, 2)
            step(V.reciprocal(st[:, 184:224], st[:, 184:224]))
            step(V.tensor_tensor(q4, q4, st[:, 184:216].unsqueeze(2).broadcast_to([P, NB * AH, HD]), ALU.mult))
            for b in range(NB):
                step(V.tensor_tensor(qn[:, b, :, :, :].rearrange("p r g d -> p g r d"),
                                     aq[:, b, :].rearrange("p (g r d) -> p g r d", g=AG, r=AR),
                                     gqk[:, 0:HD].unsqueeze(1).unsqueeze(1).broadcast_to([P, AG, AR, HD]), ALU.mult))
            step(V.tensor_tensor(k4, k4, k_rms.unsqueeze(3).broadcast_to([P, NB, AG, HD]), ALU.mult))
            V.tensor_tensor(k4, k4, gqk[:, HD:2 * HD].unsqueeze(1).unsqueeze(1).broadcast_to([P, NB, AG, HD]),
                            ALU.mult).then_inc(q_ready, 1)
            dve.wait_ge(q_ready, 1)
            take(V.tensor_scalar(iw[:, :], ready(("iw",))[:, 0:NB * IH], IDX_SCALE, None, ALU.mult))
            for b in range(NB):
                g3 = gi[:, b, :].rearrange("p (h e) -> p h e", h=HH)
                dve.wait_ge(hg_a, 6 + b)
                step(V.tensor_tensor(gi[:, b, :], gi[:, b, :], g_sig[:, b, :], ALU.mult))
                V.tensor_tensor(g3, g3, onorm[:, :].unsqueeze(1).broadcast_to([P, HH, DK]), ALU.mult).then_inc(hg_v, 1)
            dve.wait_ge(hg_v, 7 + NB)
            dve.wait_ge(filled, fills[("qT", NB - 1)] + 1)
            V.memset(state[:, 0, :, :], 0.0).then_inc(state_zero, 1)
            dve.wait_ge(state_zero, 1)
            decay = lbt[:, 16:48].rearrange("p (h n) -> p h n", h=HH)

            def ya_finish(b):
                y3 = ya[:, b, :].rearrange("p (h e) -> p h e", h=HH)
                rms = st[:, 64 + HH * b:64 + HH * (b + 1)]
                dve.wait_ge(o_roots, b + 1)
                step(V.reciprocal(rms, rms))
                step(V.tensor_tensor(y3, y3, rms.unsqueeze(2).broadcast_to([P, HH, DK]), ALU.mult))
                step(V.tensor_tensor(ya[:, b, :], ya[:, b, :], gi[:, b, :], ALU.mult))

            for n in range(NCH):
                step(V.tensor_tensor(scratch, state[:, n % 2, :, :], decay[:, :, n:n + 1].broadcast_to([P, HH, DK]),
                                     ALU.mult))
                if n:
                    dve.wait_ge(filled, fills[("o", (n - 1) // 2)] + 1)
                take(V.tensor_tensor(state[:, (n + 1) % 2, :, :], scratch,
                                     ready(("dS", n)).rearrange("p (h e) -> p h e", h=HH), ALU.add))
                fill_read(dve, ("dS", n))
                if n % 2:
                    b = n // 2
                    if b:
                        ya_finish(b - 1)
                    dve.wait_ge(o_squares, b + 1)
                    V.tensor_reduce(st[:, 64 + HH * b:64 + HH * (b + 1)],
                                    g_sig[:, b, :].rearrange("p (h e) -> p h e", h=HH), AX.X, ALU.add)\
                     .then_inc(o_sums, 1)
            ya_finish(NB - 1)
            V.memset(st[:, 249:250], 0.0).then_inc(ya_ready, 1)
            dve.wait_ge(mods_in, 16)
            ada(2)
            ada(3)
            def head_out(b, h, n):
                dve.wait_ge(p_ready, n + 1)
                step(V.reciprocal(st[:, 64 + n:65 + n], st[:, 64 + n:65 + n]))
                take(V.tensor_scalar(yb[:, b, h * HD:(h + 1) * HD], ready(("yb", b, h))[:, 0:HD],
                                     st[:, 64 + n:65 + n], None, ALU.mult))
                for key in BESIDE.get((b, h), []):
                    if key[0] == "ada":
                        ada_half(*key[1:])

            nI = n = 0
            dve.wait_ge(const, 7)
            for b in range(NB):
                W = (b + 1) * P
                if b:
                    for h in range(IH):
                        fill_read(dve, ("I", b, h))
                        weight = iw[:, b * IH + h:b * IH + h + 1]
                        if h == 0:
                            V.tensor_scalar(I_t[:, 0:W], rl[:, nI % 2, 0:W], weight, None, ALU.mult)\
                             .then_inc(relu_used, 1)
                        else:
                            V.scalar_tensor_tensor(out=I_t[:, 0:W], in0=rl[:, nI % 2, 0:W], scalar=weight,
                                                   in1=I_t[:, 0:W], op0=ALU.mult, op1=ALU.add).then_inc(relu_used, 1)
                        nI += 1
                        dve.wait_ge(relu_used, nI)
                    dve.wait_ge(i_masked, b)
                    for r in range(TOPK // 8):
                        src = I_t if r == 0 else wk
                        step(V.max(selw[:, 0:8], src[:, 0:W]))
                        step(V.match_replace(wk[:, 0:W], selw[:, 0:8], src[:, 0:W], TAKEN))
                    step(V.tensor_scalar(wk[:, 0:W], wk[:, 0:W], 0.5 * (TAKEN + FUTURE), BARRED, ALU.is_ge, ALU.mult))
                    step(V.scalar_tensor_tensor(out=dm[:, 0:W], in0=dist0[:, 0:W], scalar=float(-b * P),
                                                in1=wk[:, 0:W], op0=ALU.add, op1=ALU.add))
                else:
                    V.tensor_copy(dm[:, 0:W], dist0[:, 0:W]).then_inc(d_ready, 1)
                    dve.wait_ge(d_masked, 1)
                def masked_scores(b, h, n):
                    ps = ready(("S", b, h))
                    if n >= 2:
                        dve.wait_ge(p_ready, n - 1)
                    z = zz[:, n % 2, 0:W]
                    take(V.scalar_tensor_tensor(out=z, in0=dm[:, 0:W], scalar=2.0 ** (-8.0 * (h + 1) / AH),
                                                in1=ps[:, 0:W], op0=ALU.mult, op1=ALU.add))
                    fill_read(dve, ("S", b, h))
                    V.tensor_reduce(st[:, 16 + n:17 + n], z, AX.X, ALU.max, negate=True).then_inc(z_ready, 1)

                masked_scores(b, 0, n)
                for h in range(AH):
                    if h + 1 < AH:
                        masked_scores(b, h + 1, n + 1)
                    if h:
                        head_out(b, h - 1, n - 1)
                    n += 1
                head_out(b, AH - 1, n - 1)
            fill_read(dve, ("yb", NB - 1, AH - 1))
            V.memset(st[:, 250:251], 0.0).then_inc(yb_ready, 1)

            for b in range(NB):
                dve.wait_ge(gate_open, b + 1)
                for h in range(2):
                    part = m1[:, b, 512 * h:512 * h + 512]
                    take(V.tensor_tensor(part, part, ready(("ya_wa", b, h)), ALU.mult))
            for b in range(NB):
                dve.wait_ge(gate_open, NB + b + 1)
                for h in range(2):
                    part, other = m1[:, b, 512 * h:512 * h + 512], m2[:, b, 512 * h:512 * h + 512]
                    take(V.tensor_tensor(other, other, ready(("yb_wb", b, h)), ALU.mult))
                    fill_read(dve, ("yb_wb", b, h))
                    V.tensor_tensor(part, part, other, ALU.add).then_inc(m_ready, 1)
            dve.wait_ge(norm2_in, 16)
            fill_read(dve, ("ada", 5, 1))
            step(V.scalar_tensor_tensor(out=mods[:, 4, :], in0=mods[:, 4, :], scalar=1.0, in1=norm2,
                                        op0=ALU.add, op1=ALU.mult))

            def h2_block(b):
                dve.wait_ge(x_root, b + 2)
                step(V.reciprocal(st[:, 12 + b:13 + b], st[:, 8 + b:9 + b]))
                step(V.scalar_tensor_tensor(out=h2[:, b, :], in0=x2[:, b, :], scalar=st[:, 12 + b:13 + b],
                                            in1=mods[:, 4, :], op0=ALU.mult, op1=ALU.mult))
                V.tensor_tensor(h2[:, b, :], h2[:, b, :], mods[:, 3, :], ALU.add).then_inc(h2_ready, 1)

            dve.wait_ge(x_again, 16)
            for b in range(NB):
                for h in range(2):
                    part = x2[:, b, 512 * h:512 * h + 512]
                    take(V.tensor_tensor(ot[:, h, :], mods[:, 2, 512 * h:512 * h + 512], ready(("out", b, h)), ALU.mult))
                    fill_read(dve, ("out", b, h))
                    ins = V.tensor_tensor(part, part, ot[:, h, :], ALU.add)
                    if h == 0:
                        step(ins)
                        if b:
                            h2_block(b - 1)
                ins.then_inc(x_ready, 1)
                dve.wait_ge(x_ready, b + 1)
            h2_block(NB - 1)

            keys2 = v3(T1, 2, NKEYS, 1024)
            best = v3(T1, 2, PK, 1280)
            where_u = T1[:, 1312:1344].bitcast(u32).rearrange("p (a b) -> p a b", b=PK)
            where_f = v3(T1, 2, PK, 1344)
            top = T1[:, 1376:1392]
            pos = T1[:, 1392:1408].bitcast(u32)
            part_u = T1[:, 1408:1424].bitcast(u32)
            part_f = T1[:, 1424:1440]
            number = v3(T1, 2, PK, 1440)
            sums2 = T1[:, 1536:1792]
            picked = T1[:, 1792:2048].rearrange("p (k m) -> p k m", m=PK)
            left = T2[:, 1536:1792]

            def best16(values, numbers, src, rest):
                step_(V.max(values[:, 0:8], src))
                step_(V.max_index(numbers[:, 0:8], values[:, 0:8], src))
                step_(V.match_replace(rest, values[:, 0:8], src, TAKEN))
                step_(V.max(values[:, 8:16], rest))
                step_(V.max_index(numbers[:, 8:16], values[:, 8:16], rest))

            def key_of(half):
                step_(V.tensor_copy(part_f, part_u))
                step_(V.tensor_tensor(picked, part_f.unsqueeze(2).broadcast_to([P, PK, PK]),
                                      io16[:, :].unsqueeze(1).broadcast_to([P, PK, PK]), ALU.is_equal))
                step_(V.tensor_tensor(picked, picked, where_f[:, half:half + 1, :].broadcast_to([P, PK, PK]),
                                      ALU.mult))
                step_(V.tensor_reduce(number[:, half, :], picked, AX.X, ALU.add))

            at = [0, 0]

            def step_(ins):
                at[1] += 1
                ins.then_inc(route_step, 1)
                dve.wait_ge(route_step, at[0] + at[1])
                dve.sem_inc(step_seen, 1)

            def route(b, i):
                at[0], at[1] = i * ROUTE_STEPS, 0
                table, base = (HT, 0) if b < 2 else (AI, -4096)
                step_(V.tensor_copy(T1[:, 1024:1024 + 2 * NKEYS], table[:, bass.ds(i * (2 * NKEYS) + base, 2 * NKEYS)]))
                for j in range(2):
                    best16(best[:, j, :], where_u[:, j, :], keys2[:, j, :], left[:, 0:NKEYS])
                step_(V.tensor_copy(where_f, where_u))
                step_(V.tensor_tensor(sums2.rearrange("p (a c) -> p a c", a=PK),
                                      best[:, 0, :].unsqueeze(2).broadcast_to([P, PK, PK]),
                                      best[:, 1:2, :].broadcast_to([P, PK, PK]), ALU.add))
                best16(top, pos, sums2, left)
                V.tensor_scalar(g_now[:, :], top, top[:, 0:1], None, ALU.subtract).then_inc(route_e, 1)
                step_(V.tensor_scalar(part_u, pos, 4, None, ALU.logical_shift_right))
                key_of(0)
                step_(V.tensor_scalar(part_u, pos, PK - 1, None, ALU.bitwise_and))
                key_of(1)
                dve.wait_ge(route_x, i + 1)
                step_(V.tensor_reduce(st[:, 240:241], g_now[:, :], AX.X, ALU.add))
                step_(V.reciprocal(st[:, 241:242], st[:, 240:241]))
                step_(V.tensor_scalar(gates[:, bass.ds(i * PK, PK)], g_now[:, :], st[:, 241:242], None, ALU.mult))
                step_(V.scalar_tensor_tensor(out=ei[:, bass.ds(i * PK, PK)], in0=number[:, 0, :],
                                             scalar=float(NKEYS), in1=number[:, 1, :], op0=ALU.mult, op1=ALU.add))
                assert at[1] == ROUTE_STEPS, at[1]

            def dots(b, i):
                for k in range(PK):
                    dve.wait_ge(row_in[k], i * 32 + 16)
                    if b or k >= 2:
                        dve.wait_ge(u_used, i * PK + (k - 1))
                    V.tensor_tensor_reduce(unread[:, k % 2, :], rows[:, k, :], h2[:, b, :], 1.0, 0.0,
                                           ALU.mult, ALU.add, aw[:, k:k + 1]).then_inc(u_used, 1)
                dve.wait_ge(gelu_ready, i + 1)
                V.tensor_tensor(aw[:, 2 * PK:3 * PK], aw[:, PK:2 * PK],
                                gates[:, bass.ds(i * PK, PK)], ALU.mult).then_inc(weights_set, 1)

            for n in range(AHEAD):
                fill_read(dve, ("sc", 2 * n + 1))
                route(0, n)
            for b in range(NB):
                turn = PH * (b + 1) - AHEAD
                with dve.Fori(PH * b, turn) as i:
                    dots(b, i)
                    fill_read(dve, ("sc", 15))
                    route(b, i + AHEAD)
                with dve.Fori(turn, PH * (b + 1)) as i:
                    dots(b, i)
                    if b + 1 < NB:
                        route(b + 1, i + AHEAD)
                dve.wait_ge(summed, b + 1)
                y = x2[:, b, :].rearrange("p (a b) -> p a b", a=2)
                m = unread[:, 0, :].rearrange("p (a b) -> p a b", a=2)
                dve.wait_ge(u_used, PK * PH * (b + 1))
                for h in range(2):
                    ins = V.tensor_tensor(m[:, h, :], mods[:, 5, 512 * h:512 * h + 512], sums[:, h, :], ALU.mult)
                ins.then_inc(sums_read, 1)
                dve.wait_ge(sums_read, b + 1)
                V.tensor_tensor(y, y, m, ALU.add).then_inc(y_ready, 1)
                dve.wait_ge(y_ready, b + 1)


_INS = ["x", "c", "w_ada", "b_ada", "norm1_g", "norm2_g", "w_in", "hg_lb", "hg_onorm_g", "q_norm_g", "k_norm_g",
        "w_a", "w_b", "w_out", "peer_wq", "peer_subkeys", "peer_u", "peer_v"]


def kernel(**inputs):
    import numpy as _np
    import concourse.bacc as _bacc
    from concourse import mybir as _mybir
    from concourse.bass_utils import run_bass_kernel_spmd as _run

    nc = _bacc.Bacc("TRN2", target_bir_lowering=False, num_devices=1)
    arrays, args = {}, []
    for name in _INS:
        a = _np.ascontiguousarray(inputs[name])
        arrays[f"in_{name}"] = a
        args.append(nc.dram_tensor(f"in_{name}", a.shape, _mybir.dt.from_np(a.dtype), kind="ExternalInput").ap())
    shape = tuple(inputs["x"].shape)
    args.append(nc.dram_tensor("out_0", shape, _mybir.dt.from_np(_np.dtype("float32")), kind="ExternalOutput").ap())
    hybrid_hgrn2_dsa_peer_kernel(nc, *args)
    r = _run(nc, [arrays], core_ids=[0])
    return r.results[0]["out_0"]
```

```python
import concourse.bass as bass
from concourse import mybir
from contextlib import ExitStack


def hybrid_hgrn2_dsa_peer_kernel(
    nc, x, c, w_ada, b_ada, norm1_g, norm2_g, w_in, hg_lb, hg_onorm_g, q_norm_g, k_norm_g,
    w_a, w_b, w_out, peer_wq, peer_subkeys, peer_u, peer_v, out,
):
    fp32 = mybir.dt.float32
    u32 = mybir.dt.uint32
    ALU = mybir.AluOpType
    ACT = mybir.ActivationFunctionType
    AX = mybir.AxisListType

    P = 128
    D = x.shape[2]
    SEQ = x.shape[1]
    NB = SEQ // P
    KD = D // P
    HH, DK, CH = 4, 128, 64
    HGW = HH * DK
    NCH = SEQ // CH
    AH, AG, HD = 8, 2, 64
    AR = AH // AG
    IH = 8
    TOPK = min(256, SEQ // 4)
    PH, PK = 8, 16
    NKEYS = peer_subkeys.shape[3]
    EPS = 1e-6
    IDX_SCALE = (64 ** -0.5) * (IH ** -0.5)
    ATT_SCALE = HD ** -0.5
    TAKEN = -3.0e38
    FUTURE = -1.0e38
    BARRED = -1.0e35
    NW = 2
    RING = 16
    EARLY = 8
    ROUTE_STEPS = 32
    SHARED = 4
    AHEAD = 2
    ADA_CHUNKS = (4, 6, 8, 8, 8, 8)
    BANKS = 6
    O_Q = 0
    O_I = 2 * HGW
    O_AQ = 4 * HGW
    O_IQ = O_AQ + AH * HD + 2 * AG * HD
    O_IK = O_IQ + IH * HD
    O_IW = O_IK + HD
    O_GA = O_IW + IH
    O_GB = O_GA + D

    QUARTERS = [(s0, (s0 // CH + 1) * CH) for s0 in range(0, P, CH // 2)]

    fills, reader = {}, []

    def plan(key, engine):
        fills[key] = len(reader)
        reader.append(engine)

    for n in range(2):
        for h in range(2):
            plan(("ada", n, h), "A")
    for b in range(NB + 1):
        for h in range(2):
            if b < NB:
                plan(("hT", b, h), "A")
        for h in range(2):
            if b:
                plan(("att_in", b - 1, h), "A")
    for j in range(8):
        plan(("qf", j), "A")
    for j in range(5):
        plan(("idx_in", j), "A")
    for b in range(NB):
        for h in range(2):
            plan(("ig", b, h), "A")
    plan(("kT",), "A")
    for b in range(NB):
        plan(("qT", b), "A")
    for b in range(NB):
        plan(("kl", b), "A")
        plan(("intra", b), "A")
        plan(("dS", 2 * b), "V")
        plan(("dS", 2 * b + 1), "V")
        plan(("o", b), "A")
    for n in range(2, 4):
        for h in range(2):
            plan(("ada", n, h), "A")
    gates_left = [("ga", j) for j in range(KD)] + [("gb", j) for j in range(KD)]
    BESIDE = {}
    for place, n in (((0, -1), 1), ((0, 5), 1), ((1, -1), 3), ((1, 5), 1), ((2, -1), 3), ((2, 5), 1), ((3, -1), 4),
                     ((3, 2), 1), ((3, 5), 1)):
        BESIDE[place] = [gates_left.pop(0) for _ in range(n)]
    assert not gates_left

    def plan_beside(b, h):
        for key in BESIDE.get((b, h), []):
            plan(key, "A")

    for b in range(NB):
        if b:
            for h in range(IH):
                plan(("I", b, h), "A")
        plan(("S", b, 0), "V")
        for h in range(AH):
            if h + 1 < AH:
                plan(("S", b, h + 1), "V")
            if h == 0:
                plan_beside(b, -1)
            plan(("pT", b, h), "A")
            if h:
                plan(("yb", b, h - 1), "V")
                plan_beside(b, h - 1)
        plan(("yb", b, AH - 1), "V")
        plan_beside(b, AH - 1)
        if b == 0:
            for b2 in range(NB):
                plan(("yaT", b2), "A")
    for n in range(4, 6):
        for h in range(2):
            plan(("ada", n, h), "A")
    for j in range(KD):
        plan(("ya_wa", j), "V")
    for b in range(NB):
        plan(("ybT", b), "A")
    for j in range(KD):
        plan(("yb_wb", j), "V")
    for b in range(NB):
        for h in range(2):
            plan(("out", b, h), "V")
    for b in range(NB):
        for h in range(2):
            plan(("h2T", b, h), "A")
    for j in range(4):
        plan(("sk", j), "A")
    plan(("qry", 0), "A")
    for j in range(16):
        if j + 1 < 16:
            plan(("qry", j + 1), "A")
        plan(("sc", j), "A")

    def read_by_then(k, engine):
        return sum(e == engine for e in reader[: k + 1])

    ctx = ExitStack()
    with ctx:
        def sb(name, n, dt=fp32, parts=P):
            return ctx.enter_context(nc.sbuf_tensor(name, [parts, n], dt))

        def sem(name):
            return ctx.enter_context(nc.semaphore(name))

        PS = ctx.enter_context(nc.psum_tensor("PS", [P, 8, 512], fp32))

        XR = sb("XR", 4096)
        MODS = sb("MODS", 6144)
        WR = sb("WR", 16384)
        HT = sb("HT", 4096)
        FQ = sb("FQ", 4096)
        VG = sb("VG", 4096)
        AI = sb("AI", 5632)
        T1 = sb("T1", 2048)
        T2 = sb("T2", 2048)
        SM = sb("SM", 2048)
        ident = sb("ident", 128)
        tri = sb("tri", 512)
        dist0 = sb("dist0", 512)
        st = sb("st", 256)
        cs = sb("cs", 32)
        lbt = sb("lbt", 48)
        iw = sb("iw", NB * IH)
        gqk = sb("gqk", 2 * HD)
        selw = sb("selw", 64)
        idx_now = sb("idx_now", 32, u32)
        aw = sb("aw", 64)
        kT = sb("kT", SEQ)
        onorm = sb("onorm", DK)
        io16 = sb("io16", 16)
        g_now = sb("g_now", 16)

        def v3(t, a, b, off=0):
            return t[:, off:off + a * b].rearrange("p (a b) -> p a b", a=a)

        xt = v3(XR, NB, D)
        mods = v3(MODS, 6, D)
        hT = v3(HT, KD, SEQ)
        hq_f, hq_q = v3(FQ, HH, SEQ, 2048), v3(FQ, HH, SEQ)
        vi, gi = v3(VG, NB, HGW), v3(VG, NB, HGW, 2048)
        aq = v3(AI, NB, AH * HD)
        akv = v3(AI, NB, 2 * AG * HD, 2048)
        iqT = v3(AI, 4, SEQ, 3072)
        ikT = AI[:, 5120:5632]
        t1, t2 = v3(T1, HH, SEQ), v3(T2, HH, SEQ)
        t3, t4 = v3(XR, HH, SEQ), v3(XR, HH, SEQ, 2048)
        klT, inT = v3(SM, HH, DK), v3(SM, HH, P, 512)
        state = SM[:, 1024:2048].rearrange("p (v h e) -> p v h e", v=2, h=HH)
        ya = v3(MODS, NB, HGW)
        yb = v3(SM, NB, AH * HD)
        done_mark = st[:, 250:251]
        hbuf = v3(VG, 2, D)
        normg = T1[:, 0:D]
        junk = T1[:, D:2 * D]
        squares, k_squares = v3(SM, NB, AH * HD), v3(VG, NB, P)
        qT = v3(AI, NB * AR, P)
        qn = SM[:, 0:NB * AH * HD].rearrange("p (b r g d) -> p b r g d", b=NB, r=AR, g=AG)
        g_sig = v3(FQ, NB, HGW, 2048)
        eps, one = st[:, 248:249], st[:, 247:248]
        scratch = v3(dist0, HH, DK)
        I_t, wk, dm = VG[:, 0:512], VG[:, 512:1024], VG[:, 1024:1536]
        rl = v3(VG, 2, 512, 1536)
        zz = v3(VG, 2, 512, 2560)
        pp = v3(T2, 2, 512)
        pT = T2[:, 1024:2048].rearrange("p (v s t) -> p v s t", v=2, s=NB)
        m1, m2 = v3(XR, KD, SEQ), v3(FQ, KD, SEQ)
        x2 = v3(VG, NB, D)
        ei, gates = T2[:, 0:512].bitcast(u32), T2[:, 512:1024]
        yaT, ybT = v3(T1, 4, SEQ), v3(T2, 4, SEQ)
        h2 = v3(HT, NB, D)
        h2T = v3(FQ, KD, SEQ)
        ot = v3(AI, 2, 512, 2048)
        skn, skT = v3(T2, 16, P), v3(SM, 16, P)
        qyT = v3(T1, 2, SEQ)
        norm2 = T1[:, 1024:2048]
        zeros = T2[:, 1024:1536]
        unread = v3(MODS, 2, D)
        diag = v3(SM, PK, P)
        next_products = aw[:, 3 * PK:4 * PK]
        sums = PS[:, BANKS:BANKS + 2, :]

        w_ring = [v3(WR, KD, D, 8192 * s) for s in range(NW)]
        rows = v3(WR, RING, D)

        filled = sem("filled")
        act_read = sem("act_read")
        dve_read = sem("dve_read")
        w_loaded = [sem(f"w_loaded{s}") for s in range(NW)]
        w_half = [sem(f"w_half{n}") for n in range(2)]
        c_in = sem("c_in")
        small_in = sem("small_in")
        normg_in = sem("normg_in")
        mods_zero, bias_in = sem("mods_zero"), sem("bias_in")
        ada_terms = sem("ada_terms")
        x_in = [sem(f"x_in{b}") for b in range(NB)]
        x_again = sem("x_again")
        norm2_in = sem("norm2_in")
        sk_in = sem("sk_in")
        const = sem("const")
        v_step = sem("v_step")
        a_step = sem("a_step")
        c_exp = sem("c_exp")
        cs_ready = sem("cs_ready")
        qk_v, qk_a = sem("qk_v"), sem("qk_a")
        x_root = sem("x_root")
        h_ready = sem("h_ready")
        hg_v, hg_a = sem("hg_v"), sem("hg_a")
        f_ready = sem("f_ready")
        masked = sem("masked")
        state_zero = sem("state_zero")
        columns_set = sem("columns_set")
        o_squares, o_sums, o_roots = sem("o_squares"), sem("o_sums"), sem("o_roots")
        ya_ready = sem("ya_ready")
        gate_open = sem("gate_open")
        weights_set = sem("weights_set")
        q_ready = sem("q_ready")
        i_masked = sem("i_masked")
        d_masked = sem("d_masked")
        relu_used = sem("relu_used")
        z_ready, p_ready = sem("z_ready"), sem("p_ready")
        yb_ready = sem("yb_ready")
        m_ready = sem("m_ready")
        x_ready = sem("x_ready")
        h2_ready = sem("h2_ready")
        route_e, route_x = sem("route_e"), sem("route_x")
        route_step = sem("route_step")
        step_seen = sem("step_seen")
        idx_set = sem("idx_set")
        row_in = [sem(f"row_in{s}") for s in range(RING)]
        early_in = [sem(f"early_in{s}") for s in range(EARLY)]
        u_used = sem("u_used")
        v_used = sem("v_used")
        diag_ready = sem("diag_ready")
        summed, sums_read = sem("summed"), sem("sums_read")
        slot_free = sem("slot_free")
        gelu_ready = sem("gelu_ready")
        y_ready = sem("y_ready")
        out_done = sem("out_done")

        block = ctx.enter_context(nc.Block())

        tiles = []
        wt = {}

        def tile(name, src, slot):
            wt[name] = len(tiles)
            tiles.append((name, src, slot))

        wav = w_ada[0].rearrange("(k p) n -> p k n", p=P)
        wiv = w_in[0].rearrange("(k p) n -> p k n", p=P)
        for n in range(2):
            tile(f"ada{n}", wav[:, :, n * D:(n + 1) * D], n)
        tile("att", None, 0)
        tile("qf", wiv[:, :, O_Q:O_I], 1)
        tile("idx", None, 0)
        tile("ig", wiv[:, :, O_I:O_AQ], 1)
        for n in range(2, 4):
            tile(f"ada{n}", wav[:, :, n * D:(n + 1) * D], 0)
        tile("ga", wiv[:, :, O_GA:O_GB], 0)
        for n in range(4, 6):
            tile(f"ada{n}", wav[:, :, n * D:(n + 1) * D], 1)
        tile("gb", wiv[:, :, O_GB:O_GB + D], 1)
        tile("wab", None, 0)
        tile("wout", w_out[0].rearrange("(k p) n -> p k n", p=P), 1)
        wqv = peer_wq[0].rearrange("(k p) n -> p k n", p=P)
        tile("wq0", wqv[:, :, 0:D], 0)
        tile("wq1", wqv[:, :, D:2 * D], 1)
        parts_of = {"att": 2, "idx": 3, "wab": 2}
        last_fill = {"ada0": ("ada", 0, 1), "ada1": ("ada", 1, 1), "qf": ("qf", 7), "ig": ("ig", NB - 1, 1),
                     "att": ("att_in", NB - 1, 1), "idx": ("idx_in", 4), "ga": ("ga", KD - 1),
                     "gb": ("gb", KD - 1), "wab": ("yb_wb", KD - 1),
                     "wout": ("out", NB - 1, 1), "wq0": ("qry", 7), "wq1": ("qry", 15)}

        def wait_tile_used(eng, name):
            if name[:3] == "ada" and int(name[3]) >= 2:
                eng.wait_ge(ada_terms, sum(ADA_CHUNKS[:int(name[3]) + 1]))
            else:
                eng.wait_ge(filled, fills[last_fill[name]] + 1)

        def tile_loaded(eng, name):
            i = wt[name]
            s = tiles[i][2]
            eng.wait_ge(w_loaded[s], sum(16 * parts_of.get(t[0], 1) for t in tiles[:i + 1] if t[2] == s))
            return w_ring[s]

        def fill_read(eng, key):
            k = fills[key]
            who = reader[k]
            eng.wait_ge(act_read if who == "A" else dve_read, read_by_then(k, who))

        @block.sync
        def _(sp):
            with nc.allow_non_contiguous_dma(reason="small columns"):
                sp.dma_start(cs[:, 0:KD], c[0].rearrange("(k p) -> p k", p=P)).then_inc(c_in, 16)
                sp.dma_start(lbt[:, 0:8].rearrange("p (l h) -> p l h", l=2),
                             hg_lb.rearrange("l (h p) -> p l h", p=P)).then_inc(c_in, 16)
            for n in range(2):
                for half, signal in enumerate((w_half[n], w_loaded[n])):
                    ks = slice(half * KD // 2, (half + 1) * KD // 2)
                    sp.dma_start(w_ring[n][:, ks, :], tiles[n][1][:, ks, :]).then_inc(signal, 16)
                    if n == 0 and half == 0:
                        sp.wait_ge(mods_zero, 2)
                        sp.dma_start(MODS[0:1, :], b_ada[0:1, :]).then_inc(bias_in, 16)
            sp.dma_start(normg, norm1_g[0:1, :].to_broadcast([P, D])).then_inc(normg_in, 16)
            for b in range(NB):
                sp.dma_start(xt[:, b, :], x[0, b * P:(b + 1) * P, :]).then_inc(x_in[b], 16)
            for i in range(2, len(tiles)):
                name, src, at = tiles[i]
                wait_tile_used(sp, [t[0] for t in tiles[:i] if t[2] == at][-1])
                slot, s = w_ring[at], w_loaded[at]
                if name == "att":
                    n = AH * HD + 2 * AG * HD
                    sp.dma_start(slot[:, :, 0:n], wiv[:, :, O_AQ:O_IQ]).then_inc(s, 16)
                    sp.dma_start(slot[:, :, n:n + IH], wiv[:, :, O_IW:O_GA]).then_inc(s, 16)
                    sp.dma_start(gqk[:, 0:HD], q_norm_g[0:1, :].to_broadcast([P, HD])).then_inc(small_in, 16)
                    sp.dma_start(gqk[:, HD:2 * HD], k_norm_g[0:1, :].to_broadcast([P, HD])).then_inc(small_in, 16)
                    sp.dma_start(onorm[:, :], hg_onorm_g[0:1, :].to_broadcast([P, DK])).then_inc(small_in, 16)
                    continue
                if name == "idx":
                    n = IH * HD
                    sp.dma_start(slot[:, :, 0:n], wiv[:, :, O_IQ:O_IK]).then_inc(s, 16)
                    sp.dma_start(slot[:, :, n:n + HD], wiv[:, :, O_IK:O_IW]).then_inc(s, 16)
                    sp.dma_start(slot[:, :, n + HD:n + 2 * HD], wiv[:, :, O_IK:O_IW]).then_inc(s, 16)
                elif name == "wab":
                    sp.dma_start(slot[:, 0:4, :], w_a[0].rearrange("(k p) n -> p k n", p=P)).then_inc(s, 16)
                    sp.dma_start(slot[:, 4:8, :], w_b[0].rearrange("(k p) n -> p k n", p=P)).then_inc(s, 16)
                else:
                    sp.dma_start(slot[:, :, 0:src.shape[2]], src).then_inc(s, 16)
                if name == "wout":
                    sp.wait_ge(yb_ready, 1)
                    sp.dma_start(x2, x[0].rearrange("(b p) d -> p b d", p=P)).then_inc(x_again, 16)
                    sp.wait_ge(filled, fills[("yb_wb", KD - 1)] + 1)
                    sp.dma_start(norm2, norm2_g[0:1, :].to_broadcast([P, D])).then_inc(norm2_in, 16)
                    sp.dma_start(skn, peer_subkeys[0].rearrange("h s n d -> n (h s) d")).then_inc(sk_in, 16)
            for b in range(NB):
                for h in range(2):
                    sp.wait_ge(y_ready, 2 * b + h + 1)
                    cols = slice(512 * h, 512 * h + 512)
                    sp.dma_start(out[0, b * P:(b + 1) * P, cols], x2[:, b, cols]).then_inc(out_done, 16)
            sp.wait_ge(out_done, 16 * 2 * NB)

        @block.gpsimd
        def _(pool):
            pool.memset(MODS[:, 2 * D:6 * D], 0.0).then_inc(mods_zero, 1)
            pool.memset(ident[:, :], 0.0).then_inc(const, 1)
            pool.wait_ge(const, 1)
            pool.affine_select(out=ident[:, :], in_=ident[:, :], compare_op=ALU.not_equal, fill=1.0,
                               base=0, pattern=[[-1, P]], channel_multiplier=1).then_inc(const, 1)
            pool.memset(tri[:, :], 1.0).then_inc(const, 1)
            pool.wait_ge(const, 3)
            pool.memset(tri[:, 0:SEQ:CH], 0.0).then_inc(const, 1)
            pool.wait_ge(filled, fills[("qT", NB - 1)] + 1)
            pool.memset(inT, 0.0).then_inc(const, 1)
            pool.iota(io16[:, :], pattern=[[1, PK]], base=0, channel_multiplier=0,
                      allow_small_or_imprecise_dtypes=True).then_inc(const, 1)
            for b in range(NB):
                fill_read(pool, ("intra", b))
                pool.affine_select(out=inT, in_=inT, compare_op=ALU.is_ge, fill=0.0, base=0,
                                   pattern=[[0, HH], [1, P]], channel_multiplier=-1).then_inc(masked, 1)
            fill_read(pool, ("dS", NCH - 1))
            pool.iota(dist0[:, :], pattern=[[1, SEQ]], base=0, channel_multiplier=-1,
                      allow_small_or_imprecise_dtypes=True).then_inc(const, 1)
            pool.wait_ge(filled, fills[("o", NB - 1)] + 1)
            pool.wait_ge(const, 7)
            pool.affine_select(out=dm[:, 0:P], in_=dist0[:, 0:P], compare_op=ALU.is_ge, fill=BARRED,
                               base=0, pattern=[[-1, P]], channel_multiplier=1).then_inc(d_masked, 1)
            for b in range(1, NB):
                pool.wait_ge(relu_used, IH * b)
                last = I_t[:, b * P:(b + 1) * P]
                pool.affine_select(out=last, in_=last, compare_op=ALU.is_ge, fill=FUTURE, base=0,
                                   pattern=[[-1, P]], channel_multiplier=1).then_inc(i_masked, 1)
            pool.wait_ge(filled, fills[("sk", 3)] + 1)
            pool.memset(zeros, 0.0).then_inc(const, 1)

            def take_numbers(head, parity):
                now = idx_now[:, parity * PK:(parity + 1) * PK]
                pool.wait_ge(route_step, head * ROUTE_STEPS + ROUTE_STEPS)
                pool.sem_inc(slot_free, 1)
                pool.tensor_copy(now, ei[:, bass.ds(head * PK, PK)]).then_inc(idx_set, 1)
                pool.wait_ge(idx_set, head + 1)
                return now

            def gather(src, k, now, slot, arrived):
                pool.sem_inc(slot_free, 1)
                pool.indirect_dma_start(
                    rows[:, slot, :], None, src[0],
                    bass.IndirectOffsetOnAxis(ap=now[:, k:k + 1], axis=0)).then_inc(arrived[slot], 16)

            def gather_head(head, parity):
                now = take_numbers(head, parity)
                for src, used, n in ((peer_u, v_used, 1 - PK), (peer_v, u_used, 1)):
                    for k in range(PK):
                        pool.wait_ge(used, PK * head + k + n)
                        gather(src, k, now, k, row_in)

            numbers = [take_numbers(0, 0)]
            pool.wait_ge(filled, fills[("qry", 7)] + 1)
            for n in range(2 * PK):
                if n == PK:
                    numbers.append(take_numbers(1, 1))
                if n >= EARLY:
                    pool.wait_ge(u_used, n - EARLY + 1)
                gather(peer_u, n % PK, numbers[n // PK], n % EARLY, early_in)
            for n in range(2 * PK):
                if n < EARLY:
                    pool.wait_ge(u_used, 2 * PK - EARLY + n + 1)
                elif n == EARLY:
                    pool.wait_ge(filled, fills[("qry", 15)] + 1)
                elif n >= PK:
                    pool.wait_ge(v_used, n - PK + 1)
                gather(peer_v, n % PK, numbers[n // PK], n % PK, row_in)
            with pool.Fori(1, NB * PH // 2) as i:
                for u in range(2):
                    gather_head(2 * i + u, u)

        @block.scalar
        def _(act):
            chain = [0]

            def step(ins):
                chain[0] += 1
                ins.then_inc(a_step, 1)
                act.wait_ge(a_step, chain[0])

            def take(key, out_ap, in_ap):
                k = fills[key]
                act.wait_ge(filled, k + 1)
                nc.scalar.activation(out_ap, in_ap(PS[:, k % BANKS, :]), ACT.Copy).then_inc(act_read, 1)

            whole = lambda ps: ps
            quads = lambda ps: ps.rearrange("p (a b) -> p a b", a=4)
            act.wait_ge(c_in, 32)
            nc.scalar.activation(cs[:, KD:2 * KD], cs[:, 0:KD], ACT.Sigmoid).then_inc(c_exp, 1)
            act.wait_ge(cs_ready, 1)
            nc.scalar.activation(lbt[:, 8:16], lbt[:, 16:24], ACT.Exp).then_inc(c_exp, 1)
            act.wait_ge(columns_set, 1)

            def take_ada(n):
                for h in range(2):
                    take(("ada", n, h), mods[:, n, 512 * h:512 * h + 512], whole)

            def take_att(b):
                take(("att_in", b, 0), aq[:, b, :], whole)
                k = fills[("att_in", b, 1)]
                act.wait_ge(filled, k + 1)
                nc.scalar.activation(iw[:, b * IH:(b + 1) * IH], PS[:, k % BANKS, 2 * P:2 * P + IH], ACT.Copy,
                                     scale=IDX_SCALE)
                nc.scalar.activation(akv[:, b, :], PS[:, k % BANKS, 0:2 * P], ACT.Copy).then_inc(act_read, 1)

            take_ada(0)
            for b in range(NB):
                if b == NB - 1:
                    take_ada(1)
                act.wait_ge(x_in[b], 16)
                step(nc.scalar.activation(junk, xt[:, b, :], ACT.Square, accum_out=st[:, b:b + 1]))
            nc.scalar.activation(st[:, 8:12], st[:, 0:4], ACT.Sqrt, bias=eps, scale=1.0 / D).then_inc(x_root, 1)
            for b in range(NB + 1):
                for h in range(2):
                    if b < NB:
                        take(("hT", b, h), hT[:, 4 * h:4 * h + 4, b * P:(b + 1) * P], quads)
                if b:
                    take_att(b - 1)
            fill_read(act, ("att_in", NB - 1, 1))
            step(nc.scalar.activation(squares, aq, ACT.Square))
            nc.scalar.activation(k_squares, akv[:, :, 0:P], ACT.Square).then_inc(qk_a, 1)
            act.wait_ge(qk_v, 1)
            nc.scalar.activation(st[:, 184:224], st[:, 184:224], ACT.Sqrt).then_inc(qk_a, 1)
            for j in range(8):
                take(("qf", j), hq_q[:, j, :] if j < 4 else hq_f[:, j - 4, :], whole)
            fill_read(act, ("qf", 7))
            nc.scalar.activation(hq_f, hq_f, ACT.Sigmoid).then_inc(hg_a, 1)
            act.wait_ge(hg_v, 1)
            nc.scalar.activation(t2, hq_q, ACT.Sigmoid).then_inc(hg_a, 1)
            def take_idx(j):
                take(("idx_in", j), iqT[:, j, :] if j < 4 else ikT, whole)

            act.wait_ge(f_ready, HH)
            nc.scalar.activation(t1, hq_f, ACT.Ln).then_inc(hg_a, 1)
            take_idx(0)
            take_idx(1)
            act.wait_ge(hg_v, 3)
            step(nc.scalar.activation(t3, t1, ACT.Exp))
            step(nc.scalar.activation(t4, t2, ACT.Exp))
            nc.scalar.activation(t1, t1, ACT.Exp, scale=-1.0).then_inc(hg_a, 1)
            act.wait_ge(hg_v, 4)
            step(nc.scalar.activation(lbt[:, 16:48], st[:, 128:160], ACT.Exp))
            nc.scalar.activation(t2, t2, ACT.Exp).then_inc(hg_a, 1)
            for j in range(2, 5):
                take_idx(j)
            for b in range(NB):
                for h in range(2):
                    take(("ig", b, h), (vi, gi)[h][:, b, :], whole)
                fill_read(act, ("ig", b, 1))
                if b == 0:
                    act.wait_ge(hg_v, 7)
                nc.scalar.activation(g_sig[:, b, :], gi[:, b, :], ACT.Sigmoid).then_inc(hg_a, 1)
            take(("kT",), kT[:, :], whole)
            for b in range(NB):
                take(("qT", b), qT[:, 4 * b:4 * b + 4, :], quads)

            def root(b):
                act.wait_ge(o_sums, b + 1)
                nc.scalar.activation(st[:, 64 + HH * b:64 + HH * (b + 1)], st[:, 64 + HH * b:64 + HH * (b + 1)],
                                     ACT.Sqrt, bias=eps, scale=1.0 / DK).then_inc(o_roots, 1)

            for b in range(NB):
                if b:
                    act.wait_ge(filled, fills[("o", b - 1)] + 1)
                take(("kl", b), klT, quads)
                k = fills[("intra", b)]
                act.wait_ge(filled, k + 1)
                if b == 0:
                    act.wait_ge(const, 6)
                for s0, c1 in QUARTERS:
                    ins = nc.scalar.activation(inT[s0:s0 + CH // 2, :, s0:c1],
                                               quads(PS[s0:s0 + CH // 2, k % BANKS, :])[:, :, s0:c1], ACT.Copy)
                ins.then_inc(act_read, 1)
                if b:
                    root(b - 1)
                take(("o", b), ya[:, b, :], whole)
                if b == 0:
                    act.wait_ge(hg_v, 7 + NB)
                fill_read(act, ("o", b))
                nc.scalar.activation(g_sig[:, b, :], ya[:, b, :], ACT.Square).then_inc(o_squares, 1)
            root(NB - 1)
            take_ada(2)
            take_ada(3)
            def beside(b, h, keys=slice(None)):
                for key in BESIDE.get((b, h), [])[keys]:
                    take(key, (m1 if key[0] == "ga" else m2)[:, key[1], :], whole)

            nI = 0
            n = 0

            def exp_row(b, h, n):
                W = (b + 1) * P
                act.wait_ge(z_ready, n + 1)
                if n >= 2:
                    act.wait_ge(filled, fills[("pT", (n - 2) // AH, (n - 2) % AH)] + 1)
                nc.scalar.activation(pp[:, n % 2, 0:W], zz[:, n % 2, 0:W], ACT.Exp,
                                     bias=st[:, 16 + n:17 + n], accum_out=st[:, 64 + n:65 + n]).then_inc(p_ready, 1)

            for b in range(NB):
                W = (b + 1) * P
                if b:
                    for h in range(IH):
                        k = fills[("I", b, h)]
                        act.wait_ge(filled, k + 1)
                        if nI >= 2:
                            act.wait_ge(relu_used, nI - 1)
                        nc.scalar.activation(rl[:, nI % 2, 0:W], PS[:, k % BANKS, 0:W], ACT.Relu).then_inc(act_read, 1)
                        nI += 1
                beside(b, -1, slice(0, -1))
                exp_row(b, 0, n)
                beside(b, -1, slice(-1, None))
                for h in range(AH):
                    if h + 1 < AH:
                        exp_row(b, h + 1, n + 1)
                    if n >= 2:
                        act.wait_ge(filled, fills[("yb", (n - 2) // AH, (n - 2) % AH)] + 1)
                    take(("pT", b, h), pT[:, n % 2, 0:b + 1, :],
                         lambda ps: ps[:, 0:W].rearrange("p (a b) -> p a b", a=W // P))
                    n += 1
                    if h:
                        beside(b, h - 1)
                beside(b, AH - 1)
                if b == 0:
                    act.wait_ge(ya_ready, 1)
                    for b2 in range(NB):
                        take(("yaT", b2), yaT[:, :, b2 * P:(b2 + 1) * P], quads)
            take_ada(4)
            take_ada(5)
            fill_read(act, ("gb", KD - 1))

            def open_gates(m):
                for j in range(0, KD, 2):
                    nc.scalar.activation(m[:, j:j + 2, :], m[:, j:j + 2, :], ACT.Sigmoid).then_inc(gate_open, 1)

            open_gates(m1)
            act.wait_ge(filled, fills[("yb", NB - 1, AH - 1)] + 1)
            for b in range(NB):
                take(("ybT", b), ybT[:, :, b * P:(b + 1) * P], quads)
            open_gates(m2)
            for b in range(NB):
                act.wait_ge(x_ready, b + 1)
                step(nc.scalar.activation(T1[:, 0:D], x2[:, b, :], ACT.Square, accum_out=st[:, b:b + 1]))
                nc.scalar.activation(st[:, 8 + b:9 + b], st[:, b:b + 1], ACT.Sqrt, bias=eps,
                                     scale=1.0 / D).then_inc(x_root, 1)
            for b in range(NB):
                for h in range(2):
                    take(("h2T", b, h), h2T[:, 4 * h:4 * h + 4, b * P:(b + 1) * P], quads)
            for j in range(4):
                take(("sk", j), skT[:, 4 * j:4 * j + 4, :], quads)

            def take_q(j):
                if j == 0:
                    act.wait_ge(h2_ready, NB)
                if j >= 2:
                    act.wait_ge(filled, fills[("sc", j - 2)] + 1)
                take(("qry", j), qyT[:, j % 2, :], whole)

            def gates_exp(n):
                act.wait_ge(route_e, n)
                nc.scalar.activation(g_now[:, :], g_now[:, :], ACT.Exp).then_inc(route_x, 1)

            take_q(0)
            for j in range(16):
                if j + 1 < 16:
                    take_q(j + 1)
                if j in (4, 6):
                    gates_exp(j // 2 - 1)
                k = fills[("sc", j)]
                act.wait_ge(filled, k + 1)
                ps = quads(PS[:, k % BANKS, :])
                nc.scalar.activation(XR[:, :].rearrange("p (b j n) -> p b j n", b=2, j=16)[:, :, j, :],
                                     ps[:, 0:2, :], ACT.Copy)
                nc.scalar.activation(AI[:, 0:4096].rearrange("p (b j n) -> p b j n", b=2, j=16)[:, :, j, :],
                                     ps[:, 2:4, :], ACT.Copy).then_inc(act_read, 1)
            def weigh(i, more, products=aw[:, 0:PK]):
                act.wait_ge(u_used, i * PK + PK)
                nc.scalar.activation(aw[:, PK:2 * PK], products, ACT.Gelu).then_inc(gelu_ready, 1)
                act.wait_ge(weights_set, i + 1)
                for k in range(PK):
                    if products is next_products:
                        act.wait_ge(v_used, k + 1)
                    nc.scalar.activation(diag[:, k, :], ident[:, :], ACT.Copy,
                                         scale=aw[:, 2 * PK + k:2 * PK + k + 1]).then_inc(diag_ready, 1)
                if more:
                    gates_exp(i + (1 + AHEAD))

            weigh(0, True)
            weigh(1, True, next_products)
            with act.Fori(2, NB * PH - AHEAD) as i:
                weigh(i, True)
            with act.Fori(NB * PH - AHEAD, NB * PH) as i:
                weigh(i, False)

        @block.tensor
        def _(pe):
            def bank(key):
                k = fills[key]
                if k >= BANKS:
                    who = reader[k - BANKS]
                    pe.wait_ge(act_read if who == "A" else dve_read, read_by_then(k - BANKS, who))
                return PS[:, k % BANKS, :]

            def done(ins):
                ins.then_inc(filled, 1)

            def product(key, parts, n=512, ps=None):
                ps = bank(key) if ps is None else ps
                for i, (lhsT, rhs) in enumerate(parts):
                    ins = nc.tensor.matmul(ps[:, 0:n], lhsT, rhs, start=i == 0, stop=i == len(parts) - 1)
                return ins

            def turned(key, ins_):
                ps = bank(key)
                for i, a in enumerate(ins_):
                    last = nc.tensor.transpose(ps[:, i * P:(i + 1) * P], a, ident[:, :])
                done(last)

            pe.wait_ge(cs_ready, 2)
            pe.wait_ge(columns_set, 1)

            def ada(n):
                rest = range(ADA_CHUNKS[n], KD)
                w = tile_loaded(pe, f"ada{n}") if rest else None
                for h in range(2):
                    cols = slice(512 * h, 512 * h + 512)
                    ps = bank(("ada", n, h))
                    for k in rest:
                        nc.tensor.matmul(ps, cs[:, KD + k:KD + k + 1].broadcast_to([P, P]), w[:, k, cols],
                                         start=k == rest[0], stop=False)
                    if h == 0:
                        pe.wait_ge(ada_terms, sum(ADA_CHUNKS[:n + 1]))
                    done(nc.tensor.matmul(ps, one.broadcast_to([P, P]), mods[:, n, cols], start=not rest, stop=True))

            def token_major(key, w, src, halves, chunks=KD, k0=0, blocks=range(NB)):
                for b in blocks:
                    for h, n in enumerate(halves):
                        done(product((key, b, h), [(src[:, k, b * P:(b + 1) * P], w[:, k0 + k, 512 * h:512 * h + n])
                                                   for k in range(chunks)], n))

            ada(0)
            ada(1)
            pe.wait_ge(const, 2)
            for b in range(NB + 1):
                if b < NB:
                    pe.wait_ge(h_ready, b + 1)
                    for h in range(2):
                        turned(("hT", b, h), [hbuf[:, b % 2, (4 * h + i) * P:(4 * h + i + 1) * P] for i in range(4)])
                if b:
                    w = tile_loaded(pe, "att")
                    fill_read(pe, ("hT", b - 1, 1))
                    token_major("att_in", w, hT, (512, 2 * P + IH), blocks=[b - 1])
            w = tile_loaded(pe, "qf")
            for j in range(8):
                done(product(("qf", j), [(w[:, k, j * P:(j + 1) * P], hT[:, k, :]) for k in range(KD)]))
            w = tile_loaded(pe, "idx")
            for j in range(5):
                done(product(("idx_in", j), [(w[:, k, j * P:(j + 1) * P], hT[:, k, :]) for k in range(KD)]))
            token_major("ig", tile_loaded(pe, "ig"), hT, (512, 512))
            pe.wait_ge(q_ready, 1)
            turned(("kT",), [akv[:, b, 0:P] for b in range(NB)])
            for b in range(NB):
                turned(("qT", b), [qn[:, b, r, :, :].rearrange("p g d -> p (g d)") for r in range(AR)])
            pe.wait_ge(hg_v, 7)
            fill_read(pe, ("ig", NB - 1, 1))
            for b in range(NB):
                t = slice(b * P, (b + 1) * P)
                turned(("kl", b), [t2[:, h, t] for h in range(HH)])
                ps = bank(("intra", b))
                for h in range(HH):
                    for s0, c1 in QUARTERS:
                        last = nc.tensor.matmul(ps[s0:s0 + CH // 2, h * P + s0:h * P + c1],
                                                t1[:, h, b * P + s0:b * P + s0 + CH // 2],
                                                t3[:, h, b * P + s0:b * P + c1], start=True, stop=True)
                done(last)
                fill_read(pe, ("kl", b))
                for j in range(2):
                    ps = bank(("dS", 2 * b + j))
                    s = slice(j * CH, (j + 1) * CH)
                    for h in range(HH):
                        e = slice(h * DK, (h + 1) * DK)
                        last = nc.tensor.matmul(ps[:, e], klT[s, h, :], vi[s, b, e], start=True, stop=True)
                    done(last)
                pe.wait_ge(masked, b + 1)
                pe.wait_ge(state_zero, 1)
                fill_read(pe, ("dS", 2 * b))
                ps = bank(("o", b))
                for h in range(HH):
                    e = slice(h * DK, (h + 1) * DK)
                    nc.tensor.matmul(ps[:, e], inT[:, h, :], vi[:, b, e], start=True, stop=False)
                    nc.tensor.matmul(ps[:, e], hq_q[:, h, t], state[:, 0, h, :], start=False, stop=False)
                    last = nc.tensor.matmul(ps[:, e], t4[:, h, t], state[:, 1, h, :], start=False, stop=True)
                done(last)
            ada(2)
            ada(3)

            def beside(b, h):
                for key in BESIDE.get((b, h), []):
                    w = tile_loaded(pe, key[0])
                    done(product(key, [(w[:, k, key[1] * P:(key[1] + 1) * P], hT[:, k, :]) for k in range(KD)]))

            def att_scores(b, h):
                g, r = h // AR, h % AR
                q = qT[g * HD:(g + 1) * HD, b * AR + r, :]
                done(product(("S", b, h), [(q, kT[g * HD:(g + 1) * HD, 0:(b + 1) * P])], (b + 1) * P))

            def att_out(b, h):
                g, n = h // AR, AH * b + h
                fill_read(pe, ("pT", b, h))
                done(product(("yb", b, h), [(pT[:, n % 2, i, :], akv[:, i, P + g * HD:P + (g + 1) * HD])
                                            for i in range(b + 1)], HD))

            n = 0
            for b in range(NB):
                if b:
                    for h in range(IH):
                        s = slice((h % 2) * HD, (h % 2 + 1) * HD)
                        done(product(("I", b, h), [(iqT[s, h // 2, b * P:(b + 1) * P], ikT[s, 0:(b + 1) * P])],
                                     (b + 1) * P))
                att_scores(b, 0)
                for h in range(AH):
                    if h + 1 < AH:
                        att_scores(b, h + 1)
                    if h == 0:
                        beside(b, -1)
                    pe.wait_ge(p_ready, n + 1)
                    turned(("pT", b, h), [pp[:, n % 2, i * P:(i + 1) * P] for i in range(b + 1)])
                    if h:
                        att_out(b, h - 1)
                        beside(b, h - 1)
                    n += 1
                att_out(b, AH - 1)
                beside(b, AH - 1)
                if b == 0:
                    pe.wait_ge(ya_ready, 1)
                    for b2 in range(NB):
                        turned(("yaT", b2), [ya[:, b2, i * P:(i + 1) * P] for i in range(4)])
            ada(4)
            ada(5)
            w = tile_loaded(pe, "wab")
            fill_read(pe, ("yaT", NB - 1))

            def branch(name, src, k0):
                for j in range(KD):
                    done(product((name, j), [(w[:, k0 + k, j * P:(j + 1) * P], src[:, k, :]) for k in range(4)]))

            branch("ya_wa", yaT, 0)
            pe.wait_ge(yb_ready, 1)
            for b in range(NB):
                turned(("ybT", b), [yb[:, b, i * P:(i + 1) * P] for i in range(4)])
            fill_read(pe, ("ybT", NB - 1))
            branch("yb_wb", ybT, 4)
            w = tile_loaded(pe, "wout")
            for b in range(NB):
                for h in range(2):
                    ps = bank(("out", b, h))
                    for k in range(KD):
                        if b == 0 and h == 0:
                            pe.wait_ge(m_ready, k + 1)
                        last = nc.tensor.matmul(ps, m1[:, k, b * P:(b + 1) * P], w[:, k, 512 * h:512 * h + 512],
                                                start=k == 0, stop=k == KD - 1)
                    done(last)
            for b in range(NB):
                pe.wait_ge(h2_ready, b + 1)
                for h in range(2):
                    turned(("h2T", b, h), [h2[:, b, (4 * h + i) * P:(4 * h + i + 1) * P] for i in range(4)])
            pe.wait_ge(sk_in, 16)
            for j in range(4):
                turned(("sk", j), [skn[:, 4 * j + i, :] for i in range(4)])
            fill_read(pe, ("h2T", NB - 1, 1))

            def query(j):
                w = tile_loaded(pe, f"wq{j // 8}")
                done(product(("qry", j), [(w[:, k, (j % 8) * P:(j % 8 + 1) * P], h2T[:, k, :]) for k in range(KD)]))

            query(0)
            fill_read(pe, ("sk", 3))
            for j in range(16):
                if j + 1 < 16:
                    query(j + 1)
                fill_read(pe, ("qry", j))
                ps = bank(("sc", j))
                for b in range(NB):
                    last = nc.tensor.matmul(ps[:, b * P:(b + 1) * P], qyT[:, j % 2, b * P:(b + 1) * P], skT[:, j, :],
                                            start=True, stop=True)
                done(last)

            pe.wait_ge(const, 8)

            def add_head(i, arrived, ks=PK, ends=False):
                for k in range(ks):
                    pe.wait_ge(row_in[k], arrived)
                    pe.wait_ge(diag_ready, i * PK + (k + 1))
                    for h in range(2):
                        last = nc.tensor.matmul(sums[:, h, :], diag[:, k, :], rows[:, k, 512 * h:512 * h + 512],
                                                start=False, stop=ends and k == ks - 1)
                    last.then_inc(v_used, 1)

            for b in range(NB):
                if b:
                    pe.wait_ge(sums_read, 2 * b)
                for h in range(2):
                    nc.tensor.matmul(sums[:, h, :], zeros[:, 0:P], zeros[:, :], start=True, stop=False)
                if b == 0:
                    add_head(0, 16)
                with pe.Fori(max(1, PH * b), min(PH * (b + 1), NB * PH - 1)) as i:
                    add_head(i, i * 32)
                if b + 1 < NB:
                    for h in range(2):
                        last = nc.tensor.matmul(sums[:, h, :], zeros[:, 0:P], zeros[:, :], start=False, stop=True)
                    last.then_inc(summed, 1)
            add_head(NB * PH - 1, (NB * PH - 1) * 32, PK - SHARED, ends=True)

        @block.vector
        def _(dve):
            V = nc.vector
            chain = [0]

            def step(ins):
                chain[0] += 1
                ins.then_inc(v_step, 1)
                dve.wait_ge(v_step, chain[0])

            def ready(key):
                k = fills[key]
                dve.wait_ge(filled, k + 1)
                return PS[:, k % BANKS, :]

            def take(ins):
                ins.then_inc(dve_read, 1)

            V.memset(eps, EPS)
            V.memset(one, 1.0).then_inc(columns_set, 1)
            V.memset(MODS[:, 0:2 * D], 0.0).then_inc(mods_zero, 1)
            dve.wait_ge(c_in, 32)
            step(V.tensor_tensor(lbt[:, 40:44], lbt[:, 0:4], lbt[:, 4:8], ALU.max))
            V.tensor_tensor(lbt[:, 16:24].rearrange("p (l h) -> p l h", l=2),
                            lbt[:, 0:8].rearrange("p (l h) -> p l h", l=2),
                            lbt[:, 40:44].unsqueeze(1).broadcast_to([P, 2, 4]), ALU.subtract).then_inc(cs_ready, 1)
            dve.wait_ge(c_exp, 1)
            V.tensor_tensor(cs[:, KD:2 * KD], cs[:, KD:2 * KD], cs[:, 0:KD], ALU.mult).then_inc(cs_ready, 1)
            dve.wait_ge(c_exp, 2)
            step(V.tensor_tensor(lbt[:, 16:20], lbt[:, 8:12], lbt[:, 12:16], ALU.add))
            step(V.reciprocal(lbt[:, 16:20], lbt[:, 16:20]))
            step(V.tensor_tensor(lbt[:, 0:4], lbt[:, 8:12], lbt[:, 16:20], ALU.mult))
            step(V.tensor_scalar(lbt[:, 4:8], lbt[:, 0:4], -1.0, 1.0, ALU.mult, ALU.add))
            def add_ada(n, k):
                if k == 0 and n < 2:
                    dve.wait_ge(w_half[n], 16)
                elif k == 0 or n < 2 and k == KD // 2:
                    tile_loaded(dve, f"ada{n}")
                if n or k:
                    dve.wait_ge(ada_terms, sum(ADA_CHUNKS[:n]) + k)
                V.scalar_tensor_tensor(out=mods[:, n, :], in0=w_ring[tiles[wt[f"ada{n}"]][2]][:, k, :],
                                       scalar=cs[:, KD + k:KD + k + 1], in1=mods[:, n, :],
                                       op0=ALU.mult, op1=ALU.add).then_inc(ada_terms, 1)

            dve.wait_ge(bias_in, 16)
            dve.wait_ge(cs_ready, 2)
            for n in range(2):
                for k in range(ADA_CHUNKS[n]):
                    add_ada(n, k)
            dve.wait_ge(normg_in, 16)
            fill_read(dve, ("ada", 1, 1))
            step(V.scalar_tensor_tensor(out=mods[:, 1, :], in0=mods[:, 1, :], scalar=1.0, in1=normg,
                                        op0=ALU.add, op1=ALU.mult))
            dve.wait_ge(x_root, 1)
            step(V.reciprocal(st[:, 12:16], st[:, 8:12]))
            for b in range(NB):
                if b >= 2:
                    dve.wait_ge(filled, fills[("hT", b - 2, 1)] + 1)
                step(V.scalar_tensor_tensor(out=hbuf[:, b % 2, :], in0=xt[:, b, :], scalar=st[:, 12 + b:13 + b],
                                            in1=mods[:, 1, :], op0=ALU.mult, op1=ALU.mult))
                V.tensor_tensor(hbuf[:, b % 2, :], hbuf[:, b % 2, :], mods[:, 0, :], ALU.add).then_inc(h_ready, 1)
            dve.wait_ge(h_ready, NB)
            V.memset(done_mark, 0.0).then_inc(hg_v, 1)
            q4 = aq.rearrange("p b (h e) -> p (b h) e", h=AH)
            k4 = akv[:, :, 0:P].rearrange("p b (g d) -> p b g d", g=AG)
            k_rms = st[:, 216:224].rearrange("p (b g) -> p b g", b=NB)
            dve.wait_ge(qk_a, 1)
            step(V.tensor_reduce(st[:, 184:216], squares.rearrange("p b (h e) -> p (b h) e", h=AH), AX.X, ALU.add))
            step(V.tensor_reduce(k_rms, k_squares.rearrange("p b (g e) -> p b g e", g=AG), AX.X, ALU.add))
            V.tensor_scalar(st[:, 184:224], st[:, 184:224], 1.0 / HD, EPS, ALU.mult, ALU.add).then_inc(qk_v, 1)
            dve.wait_ge(small_in, 48)
            step(V.tensor_scalar(gqk[:, 0:HD], gqk[:, 0:HD], ATT_SCALE, None, ALU.mult))
            dve.wait_ge(qk_a, 2)
            step(V.reciprocal(st[:, 184:224], st[:, 184:224]))
            step(V.tensor_tensor(q4, q4, st[:, 184:216].unsqueeze(2).broadcast_to([P, NB * AH, HD]), ALU.mult))
            for b in range(NB):
                step(V.tensor_tensor(qn[:, b, :, :, :].rearrange("p r g d -> p g r d"),
                                     aq[:, b, :].rearrange("p (g r d) -> p g r d", g=AG, r=AR),
                                     gqk[:, 0:HD].unsqueeze(1).unsqueeze(1).broadcast_to([P, AG, AR, HD]), ALU.mult))
            step(V.tensor_tensor(k4, k4, k_rms.unsqueeze(3).broadcast_to([P, NB, AG, HD]), ALU.mult))
            V.tensor_tensor(k4, k4, gqk[:, HD:2 * HD].unsqueeze(1).unsqueeze(1).broadcast_to([P, NB, AG, HD]),
                            ALU.mult).then_inc(q_ready, 1)
            dve.wait_ge(hg_a, 1)
            for h in range(HH):
                V.tensor_scalar(hq_f[:, h, :], hq_f[:, h, :], lbt[:, 4 + h:5 + h], lbt[:, h:h + 1],
                                ALU.mult, ALU.add).then_inc(f_ready, 1)
            dve.wait_ge(hg_a, 2)
            V.tensor_tensor(hq_q, hq_q, t2, ALU.mult).then_inc(hg_v, 1)
            dve.wait_ge(hg_v, 2)
            dve.wait_ge(hg_a, 3)
            step(V.tensor_scalar(hq_f, hq_f, -1.0, 1.0, ALU.mult, ALU.add))
            dve.wait_ge(const, 4)
            for h in range(HH):
                step(V.tensor_tensor_scan(t2[:, h, :], tri[:, :], t1[:, h, :], 0.0, ALU.mult, ALU.add))
            chunks = lambda t: t.rearrange("p h (n c) -> p (h n) c", c=CH)
            bl = st[:, 128:160]
            bm = st[:, 96:128]
            step(V.tensor_copy(bl.unsqueeze(2), chunks(t2)[:, :, CH - 1:CH]))
            step(V.tensor_copy(bm.unsqueeze(2), chunks(t2)[:, :, CH // 2 - 1:CH // 2]))
            V.tensor_tensor(chunks(t1), chunks(t2), bm.unsqueeze(2).broadcast_to([P, HH * NCH, CH]),
                            ALU.subtract).then_inc(hg_v, 1)
            dve.wait_ge(hg_a, 4)
            V.tensor_tensor(chunks(t2), bl.unsqueeze(2).broadcast_to([P, HH * NCH, CH]), chunks(t2),
                            ALU.subtract).then_inc(hg_v, 1)
            V.tensor_tensor(t1, hq_f, t1, ALU.mult).then_inc(hg_v, 1)
            step(V.tensor_tensor(t3, hq_q, t3, ALU.mult))
            step(V.tensor_tensor(t4, hq_q, t4, ALU.mult))
            even = lambda t: t.rearrange("p h (n j c) -> p (h n) j c", j=2, c=CH)[:, :, 0, :]
            odd = lambda t: t.rearrange("p h (n j c) -> p (h n) j c", j=2, c=CH)[:, :, 1, :]
            step(V.tensor_copy(even(hq_q), even(t4)))
            step(V.memset(odd(hq_q), 0.0))
            V.memset(even(t4), 0.0).then_inc(hg_v, 1)
            dve.wait_ge(hg_a, 5)
            V.tensor_tensor(t2, hq_f, t2, ALU.mult).then_inc(hg_v, 1)
            for n in range(2, 4):
                for k in range(KD):
                    add_ada(n, k)
            for b in range(NB):
                g3 = gi[:, b, :].rearrange("p (h e) -> p h e", h=HH)
                dve.wait_ge(hg_a, 6 + b)
                step(V.tensor_tensor(gi[:, b, :], gi[:, b, :], g_sig[:, b, :], ALU.mult))
                V.tensor_tensor(g3, g3, onorm[:, :].unsqueeze(1).broadcast_to([P, HH, DK]), ALU.mult).then_inc(hg_v, 1)
            dve.wait_ge(hg_v, 7 + NB)
            dve.wait_ge(filled, fills[("qT", NB - 1)] + 1)
            V.memset(state[:, 0, :, :], 0.0).then_inc(state_zero, 1)
            dve.wait_ge(state_zero, 1)
            decay = lbt[:, 16:48].rearrange("p (h n) -> p h n", h=HH)

            def ya_finish(b):
                y3 = ya[:, b, :].rearrange("p (h e) -> p h e", h=HH)
                rms = st[:, 64 + HH * b:64 + HH * (b + 1)]
                dve.wait_ge(o_roots, b + 1)
                step(V.reciprocal(rms, rms))
                step(V.tensor_tensor(y3, y3, rms.unsqueeze(2).broadcast_to([P, HH, DK]), ALU.mult))
                step(V.tensor_tensor(ya[:, b, :], ya[:, b, :], gi[:, b, :], ALU.mult))

            for n in range(NCH):
                step(V.tensor_tensor(scratch, state[:, n % 2, :, :], decay[:, :, n:n + 1].broadcast_to([P, HH, DK]),
                                     ALU.mult))
                if n:
                    dve.wait_ge(filled, fills[("o", (n - 1) // 2)] + 1)
                take(V.tensor_tensor(state[:, (n + 1) % 2, :, :], scratch,
                                     ready(("dS", n)).rearrange("p (h e) -> p h e", h=HH), ALU.add))
                fill_read(dve, ("dS", n))
                if n % 2:
                    b = n // 2
                    if b:
                        ya_finish(b - 1)
                    dve.wait_ge(o_squares, b + 1)
                    V.tensor_reduce(st[:, 64 + HH * b:64 + HH * (b + 1)],
                                    g_sig[:, b, :].rearrange("p (h e) -> p h e", h=HH), AX.X, ALU.add)\
                     .then_inc(o_sums, 1)
            ya_finish(NB - 1)
            V.memset(done_mark, 0.0).then_inc(ya_ready, 1)
            def head_out(b, h, n):
                dve.wait_ge(p_ready, n + 1)
                step(V.reciprocal(st[:, 64 + n:65 + n], st[:, 64 + n:65 + n]))
                take(V.tensor_scalar(yb[:, b, h * HD:(h + 1) * HD], ready(("yb", b, h))[:, 0:HD],
                                     st[:, 64 + n:65 + n], None, ALU.mult))

            nI = n = 0
            dve.wait_ge(const, 7)
            for b in range(NB):
                W = (b + 1) * P
                if b:
                    for h in range(IH):
                        fill_read(dve, ("I", b, h))
                        weight = iw[:, b * IH + h:b * IH + h + 1]
                        if h == 0:
                            V.tensor_scalar(I_t[:, 0:W], rl[:, nI % 2, 0:W], weight, None, ALU.mult)\
                             .then_inc(relu_used, 1)
                        else:
                            V.scalar_tensor_tensor(out=I_t[:, 0:W], in0=rl[:, nI % 2, 0:W], scalar=weight,
                                                   in1=I_t[:, 0:W], op0=ALU.mult, op1=ALU.add).then_inc(relu_used, 1)
                        nI += 1
                        dve.wait_ge(relu_used, nI)
                    dve.wait_ge(i_masked, b)
                    for r in range(TOPK // 8):
                        src = I_t if r == 0 else wk
                        step(V.max(selw[:, 0:8], src[:, 0:W]))
                        step(V.match_replace(wk[:, 0:W], selw[:, 0:8], src[:, 0:W], TAKEN))
                    step(V.tensor_scalar(wk[:, 0:W], wk[:, 0:W], 0.5 * (TAKEN + FUTURE), BARRED, ALU.is_ge, ALU.mult))
                    step(V.scalar_tensor_tensor(out=dm[:, 0:W], in0=dist0[:, 0:W], scalar=float(-b * P),
                                                in1=wk[:, 0:W], op0=ALU.add, op1=ALU.add))
                else:
                    dve.wait_ge(d_masked, 1)
                def masked_scores(b, h, n):
                    ps = ready(("S", b, h))
                    if n >= 2:
                        dve.wait_ge(p_ready, n - 1)
                    z = zz[:, n % 2, 0:W]
                    take(V.scalar_tensor_tensor(out=z, in0=dm[:, 0:W], scalar=2.0 ** (-8.0 * (h + 1) / AH),
                                                in1=ps[:, 0:W], op0=ALU.mult, op1=ALU.add))
                    fill_read(dve, ("S", b, h))
                    V.tensor_reduce(st[:, 16 + n:17 + n], z, AX.X, ALU.max, negate=True).then_inc(z_ready, 1)

                masked_scores(b, 0, n)
                for h in range(AH):
                    if h + 1 < AH:
                        masked_scores(b, h + 1, n + 1)
                    if h:
                        head_out(b, h - 1, n - 1)
                    if b < 2:
                        add_ada(4 + b, h)
                    n += 1
                head_out(b, AH - 1, n - 1)
            fill_read(dve, ("yb", NB - 1, AH - 1))
            V.memset(done_mark, 0.0).then_inc(yb_ready, 1)

            for j in range(KD):
                dve.wait_ge(gate_open, j // 2 + 1)
                take(V.tensor_tensor(m1[:, j, :], m1[:, j, :], ready(("ya_wa", j)), ALU.mult))
            for j in range(KD):
                dve.wait_ge(gate_open, KD // 2 + j // 2 + 1)
                take(V.tensor_tensor(m2[:, j, :], m2[:, j, :], ready(("yb_wb", j)), ALU.mult))
                fill_read(dve, ("yb_wb", j))
                V.tensor_tensor(m1[:, j, :], m1[:, j, :], m2[:, j, :], ALU.add).then_inc(m_ready, 1)
            dve.wait_ge(norm2_in, 16)
            fill_read(dve, ("ada", 5, 1))
            step(V.scalar_tensor_tensor(out=mods[:, 4, :], in0=mods[:, 4, :], scalar=1.0, in1=norm2,
                                        op0=ALU.add, op1=ALU.mult))

            def h2_block(b):
                dve.wait_ge(x_root, b + 2)
                step(V.reciprocal(st[:, 12 + b:13 + b], st[:, 8 + b:9 + b]))
                step(V.scalar_tensor_tensor(out=h2[:, b, :], in0=x2[:, b, :], scalar=st[:, 12 + b:13 + b],
                                            in1=mods[:, 4, :], op0=ALU.mult, op1=ALU.mult))
                V.tensor_tensor(h2[:, b, :], h2[:, b, :], mods[:, 3, :], ALU.add).then_inc(h2_ready, 1)

            dve.wait_ge(x_again, 16)
            for b in range(NB):
                for h in range(2):
                    part = x2[:, b, 512 * h:512 * h + 512]
                    take(V.tensor_tensor(ot[:, h, :], mods[:, 2, 512 * h:512 * h + 512], ready(("out", b, h)),
                                         ALU.mult))
                    fill_read(dve, ("out", b, h))
                    ins = V.tensor_tensor(part, part, ot[:, h, :], ALU.add)
                    if h == 0:
                        step(ins)
                        if b:
                            h2_block(b - 1)
                ins.then_inc(x_ready, 1)
                dve.wait_ge(x_ready, b + 1)
            h2_block(NB - 1)

            keys2 = v3(T1, 2, NKEYS, 1024)
            best = v3(T1, 2, PK, 1280)
            where_u = T1[:, 1312:1344].bitcast(u32).rearrange("p (a b) -> p a b", b=PK)
            where_f = v3(T1, 2, PK, 1344)
            top = T1[:, 1376:1392]
            pos = T1[:, 1392:1408].bitcast(u32)
            part_u = T1[:, 1408:1424].bitcast(u32)
            part_f = T1[:, 1424:1440]
            number = v3(T1, 2, PK, 1440)
            sums2 = T1[:, 1536:1792]
            picked = T1[:, 1792:2048].rearrange("p (k m) -> p k m", m=PK)
            left = T2[:, 1536:1792]

            def best16(values, numbers, src, rest):
                step_(V.max(values[:, 0:8], src))
                step_(V.max_index(numbers[:, 0:8], values[:, 0:8], src))
                step_(V.match_replace(rest, values[:, 0:8], src, TAKEN))
                step_(V.max(values[:, 8:16], rest))
                step_(V.max_index(numbers[:, 8:16], values[:, 8:16], rest))

            def key_of(half):
                step_(V.tensor_copy(part_f, part_u))
                step_(V.tensor_tensor(picked, part_f.unsqueeze(2).broadcast_to([P, PK, PK]),
                                      io16[:, :].unsqueeze(1).broadcast_to([P, PK, PK]), ALU.is_equal))
                step_(V.tensor_tensor(picked, picked, where_f[:, half:half + 1, :].broadcast_to([P, PK, PK]),
                                      ALU.mult))
                step_(V.tensor_reduce(number[:, half, :], picked, AX.X, ALU.add))

            at = [0, 0]

            def step_(ins):
                at[1] += 1
                ins.then_inc(route_step, 1)
                dve.wait_ge(route_step, at[0] + at[1])
                dve.sem_inc(step_seen, 1)

            def route(b, i):
                at[0], at[1] = i * ROUTE_STEPS, 0
                table, base = (XR, 0) if b < 2 else (AI, -4096)
                step_(V.tensor_copy(T1[:, 1024:1024 + 2 * NKEYS], table[:, bass.ds(i * (2 * NKEYS) + base, 2 * NKEYS)]))
                for j in range(2):
                    best16(best[:, j, :], where_u[:, j, :], keys2[:, j, :], left[:, 0:NKEYS])
                step_(V.tensor_copy(where_f, where_u))
                step_(V.tensor_tensor(sums2.rearrange("p (a c) -> p a c", a=PK),
                                      best[:, 0, :].unsqueeze(2).broadcast_to([P, PK, PK]),
                                      best[:, 1:2, :].broadcast_to([P, PK, PK]), ALU.add))
                best16(top, pos, sums2, left)
                V.tensor_scalar(g_now[:, :], top, top[:, 0:1], None, ALU.subtract).then_inc(route_e, 1)
                step_(V.tensor_scalar(part_u, pos, 4, None, ALU.logical_shift_right))
                key_of(0)
                step_(V.tensor_scalar(part_u, pos, PK - 1, None, ALU.bitwise_and))
                key_of(1)
                dve.wait_ge(route_x, i + 1)
                step_(V.tensor_reduce(st[:, 240:241], g_now[:, :], AX.X, ALU.add))
                step_(V.reciprocal(st[:, 241:242], st[:, 240:241]))
                step_(V.tensor_scalar(gates[:, bass.ds(i * PK, PK)], g_now[:, :], st[:, 241:242], None, ALU.mult))
                step_(V.scalar_tensor_tensor(out=ei[:, bass.ds(i * PK, PK)], in0=number[:, 0, :],
                                             scalar=float(NKEYS), in1=number[:, 1, :], op0=ALU.mult, op1=ALU.add))
                assert at[1] == ROUTE_STEPS, at[1]

            def dots(b, i, arrived, slots=PK, signals=row_in, products=aw[:, 0:PK], first=False):
                for k in range(PK):
                    slot = k % slots
                    dve.wait_ge(signals[slot], arrived + 16 * (k // slots))
                    if k >= 2 or not first:
                        dve.wait_ge(u_used, i * PK + (k - 1))
                    V.tensor_tensor_reduce(unread[:, k % 2, :], rows[:, slot, :], h2[:, b, :], 1.0, 0.0,
                                           ALU.mult, ALU.add, products[:, k:k + 1]).then_inc(u_used, 1)

            def weights(i):
                dve.wait_ge(gelu_ready, i + 1)
                V.tensor_tensor(aw[:, 2 * PK:3 * PK], aw[:, PK:2 * PK],
                                gates[:, bass.ds(i * PK, PK)], ALU.mult).then_inc(weights_set, 1)

            for n in range(AHEAD):
                fill_read(dve, ("sc", 2 * n + 1))
                route(0, n)
            for b in range(NB):
                turn = PH * (b + 1) - AHEAD
                if b == 0:
                    dots(0, 0, 16, EARLY, early_in, first=True)
                    dots(0, 1, 16 + 16 * PK // EARLY, EARLY, early_in, next_products)
                    fill_read(dve, ("sc", 15))
                    for i in range(2):
                        weights(i)
                        route(0, i + AHEAD)
                with dve.Fori(max(2, PH * b), turn) as i:
                    dots(b, i, i * 32 - 16)
                    weights(i)
                    route(b, i + AHEAD)
                with dve.Fori(turn, PH * (b + 1)) as i:
                    dots(b, i, i * 32 - 16)
                    weights(i)
                    if b + 1 < NB:
                        route(b + 1, i + AHEAD)
                if b == NB - 1:
                    head = NB * PH - 1
                    part = unread[:, 1, :]
                    dve.wait_ge(u_used, PK * NB * PH)
                    dve.wait_ge(weights_set, NB * PH)
                    for k in range(PK - SHARED, PK):
                        dve.wait_ge(row_in[k], head * 32)
                        w = aw[:, 2 * PK + k:2 * PK + k + 1]
                        if k == PK - SHARED:
                            step(V.tensor_scalar(part, rows[:, k, :], w, None, ALU.mult))
                        else:
                            step(V.scalar_tensor_tensor(out=part, in0=rows[:, k, :], scalar=w, in1=part,
                                                        op0=ALU.mult, op1=ALU.add))
                    step(V.tensor_tensor(part, part, mods[:, 5, :], ALU.mult))
                    step(V.tensor_tensor(x2[:, b, :], x2[:, b, :], part, ALU.add))
                if b + 1 < NB:
                    dve.wait_ge(summed, b + 1)
                else:
                    dve.wait_ge(v_used, PK * NB * PH - SHARED)
                y = x2[:, b, :].rearrange("p (a b) -> p a b", a=2)
                m = unread[:, 0, :].rearrange("p (a b) -> p a b", a=2)
                dve.wait_ge(u_used, PK * PH * (b + 1))
                for h in range(2):
                    V.tensor_tensor(m[:, h, :], mods[:, 5, 512 * h:512 * h + 512], sums[:, h, :], ALU.mult)\
                     .then_inc(sums_read, 1)
                    dve.wait_ge(sums_read, 2 * b + h + 1)
                    V.tensor_tensor(y[:, h, :], y[:, h, :], m[:, h, :], ALU.add).then_inc(y_ready, 1)
                dve.wait_ge(y_ready, 2 * (b + 1))


_INS = ["x", "c", "w_ada", "b_ada", "norm1_g", "norm2_g", "w_in", "hg_lb", "hg_onorm_g", "q_norm_g", "k_norm_g",
        "w_a", "w_b", "w_out", "peer_wq", "peer_subkeys", "peer_u", "peer_v"]


def kernel(**inputs):
    import numpy as _np
    import concourse.bacc as _bacc
    from concourse import mybir as _mybir
    from concourse.bass_utils import run_bass_kernel_spmd as _run

    nc = _bacc.Bacc("TRN2", target_bir_lowering=False, num_devices=1)
    arrays, args = {}, []
    for name in _INS:
        a = _np.ascontiguousarray(inputs[name])
        arrays[f"in_{name}"] = a
        args.append(nc.dram_tensor(f"in_{name}", a.shape, _mybir.dt.from_np(a.dtype), kind="ExternalInput").ap())
    shape = tuple(inputs["x"].shape)
    args.append(nc.dram_tensor("out_0", shape, _mybir.dt.from_np(_np.dtype("float32")), kind="ExternalOutput").ap())
    hybrid_hgrn2_dsa_peer_kernel(nc, *args)
    r = _run(nc, [arrays], core_ids=[0])
    return r.results[0]["out_0"]
```
